# Optimizing a Trainium2 kernel written in Bass

```python
import math
import jax, jax.numpy as jnp
from jax import lax
import numpy as np

D_MODEL = 1024
BATCH = 1
SEQ = 256
DEPTH = 2

HEAD_DIM = 64
BLOCK = 128
LRU_WIDTH = D_MODEL // 2
LRU_BLOCKS = 8
LRU_BLOCK = LRU_WIDTH // LRU_BLOCKS
CONV_WIDTH = 4
LRU_C = 8.0
FOX_HEADS = (D_MODEL // 2) // HEAD_DIM
DIL_HEADS = (D_MODEL // 2) // HEAD_DIM
DIL_PATTERN = ((128, 1), (512, 4), (2048, 16))
SWA_Q_HEADS = (D_MODEL // 2) // HEAD_DIM
SWA_KV_HEADS = 2
SWA_WINDOW = 128
MEM_LEN = 256
XA_HEADS = 4
XA_HEAD_DIM = D_MODEL // XA_HEADS
D_FF = 4 * D_MODEL
ROPE_THETA = 10000.0
EPS = 1e-6

N_EVEN = (DEPTH + 1) // 2
N_ODD = DEPTH // 2
FOX_W = FOX_HEADS * HEAD_DIM
DIL_W = DIL_HEADS * HEAD_DIM
SWA_QW = SWA_Q_HEADS * HEAD_DIM
SWA_KW = SWA_KV_HEADS * HEAD_DIM
AB_IN = 2 * LRU_WIDTH + 3 * FOX_W + FOX_HEADS
AB_MIX = LRU_WIDTH + FOX_W
CD_IN = 3 * DIL_W + SWA_QW + 2 * SWA_KW
CD_MIX = DIL_W + SWA_QW


def rmsnorm(x, g):
    xf = x.astype(jnp.float32)
    y = xf * lax.rsqrt(jnp.mean(xf * xf, axis=-1, keepdims=True) + EPS)
    return (y * g.astype(jnp.float32)).astype(x.dtype)

def rope(x, pos):
    half = x.shape[-1] // 2
    inv = ROPE_THETA ** (-jnp.arange(half, dtype=jnp.float32) / half)
    ang = pos.astype(jnp.float32)[:, None] * inv[None, :]
    cos = jnp.cos(ang)[None, :, None, :]
    sin = jnp.sin(ang)[None, :, None, :]
    xf = x.astype(jnp.float32)
    x1, x2 = xf[..., :half], xf[..., half:]
    return jnp.concatenate([x1 * cos - x2 * sin, x2 * cos + x1 * sin], axis=-1).astype(x.dtype)

def causal_depthwise_conv(u, w, b):
    out = lax.conv_general_dilated(
        u, w[:, None, :].astype(u.dtype), window_strides=(1,),
        padding=[(CONV_WIDTH - 1, 0)], dimension_numbers=("NWC", "WIO", "NWC"),
        feature_group_count=u.shape[-1])
    return out + b.astype(u.dtype)

def _linear_recurrence_combine(e1, e2):
    a1, b1 = e1
    a2, b2 = e2
    return a1 * a2, a2 * b1 + b2

def rg_lru(u, w_a, b_a, w_i, b_i, lam):
    bsz, s, c = u.shape
    uf = u.astype(jnp.float32)
    ub = uf.reshape(bsz, s, LRU_BLOCKS, LRU_BLOCK)
    r = jax.nn.sigmoid(jnp.einsum("bsgc,gcd->bsgd", ub, w_a.astype(jnp.float32)).reshape(bsz, s, c) + b_a.astype(jnp.float32))
    i = jax.nn.sigmoid(jnp.einsum("bsgc,gcd->bsgd", ub, w_i.astype(jnp.float32)).reshape(bsz, s, c) + b_i.astype(jnp.float32))
    log_a = -LRU_C * r * jax.nn.softplus(-lam.astype(jnp.float32))
    a = jnp.exp(log_a)
    x_in = jnp.sqrt(-jnp.expm1(2.0 * log_a)) * (i * uf)
    _, h = lax.associative_scan(_linear_recurrence_combine, (a, x_in), axis=1)
    return h.astype(u.dtype)

def forgetting_attention(q, k, v, log_f):
    s_len = q.shape[1]
    scale = q.shape[-1] ** -0.5
    c = jnp.cumsum(log_f, axis=1).transpose(0, 2, 1)
    outs = []
    for blk in range(s_len // BLOCK):
        q0, q1 = blk * BLOCK, (blk + 1) * BLOCK
        sc = jnp.einsum("bqhd,bkhd->bhqk", q[:, q0:q1], k[:, :q1]).astype(jnp.float32) * scale
        bias = c[:, :, q0:q1, None] - c[:, :, None, :q1]
        mask = jnp.arange(q0, q1)[:, None] >= jnp.arange(q1)[None, :]
        p = jax.nn.softmax(jnp.where(mask, sc + bias, -jnp.inf), axis=-1)
        outs.append(jnp.einsum("bhqk,bkhd->bqhd", p, v[:, :q1].astype(jnp.float32)))
    return jnp.concatenate(outs, axis=1).astype(q.dtype)

def banded_partial(q, k, v, max_dist):
    n, l, hk, g, dh = q.shape
    nb = -(-l // BLOCK)
    lp = nb * BLOCK
    pad = lp - l
    qb = jnp.pad(q, ((0, 0), (0, pad), (0, 0), (0, 0), (0, 0))).reshape(n, nb, BLOCK, hk, g, dh)
    kp = jnp.pad(k, ((0, 0), (BLOCK, pad), (0, 0), (0, 0))).reshape(n, nb + 1, BLOCK, hk, dh)
    vp = jnp.pad(v, ((0, 0), (BLOCK, pad), (0, 0), (0, 0))).reshape(n, nb + 1, BLOCK, hk, dh)
    kb = jnp.concatenate([kp[:, :-1], kp[:, 1:]], axis=2)
    vb = jnp.concatenate([vp[:, :-1], vp[:, 1:]], axis=2)
    sc = jnp.einsum("nbqhgd,nbkhd->nbhgqk", qb, kb).astype(jnp.float32) * dh ** -0.5
    qpos = jnp.arange(BLOCK)[:, None] + BLOCK
    kpos = jnp.arange(2 * BLOCK)[None, :]
    dist = qpos - kpos
    blk = jnp.arange(nb)[:, None, None]
    valid = (dist >= 0) & (dist <= max_dist) & (blk * BLOCK - BLOCK + kpos >= 0)
    sc = jnp.where(valid[None, :, None, None], sc, -jnp.inf)
    m = jnp.max(sc, axis=-1)
    p = jnp.exp(sc - m[..., None])
    den = jnp.sum(p, axis=-1)
    num = jnp.einsum("nbhgqk,nbkhd->nbqhgd", p, vb.astype(jnp.float32)).reshape(n, lp, hk, g, dh)[:, :l]
    m = m.transpose(0, 1, 4, 2, 3).reshape(n, lp, hk, g)[:, :l]
    den = den.transpose(0, 1, 4, 2, 3).reshape(n, lp, hk, g)[:, :l]
    return num, m, den

def dilated_attention(q, k, v):
    bsz, s, h, dh = q.shape
    nums, ms, dens = [], [], []
    for window, dil in DIL_PATTERN:
        l = s // dil

        def to_classes(t):
            return t.reshape(bsz, l, dil, h, dh).transpose(0, 2, 1, 3, 4).reshape(bsz * dil, l, h, dh)

        num, m, den = banded_partial(to_classes(q)[:, :, :, None, :], to_classes(k), to_classes(v), window // dil)
        nums.append(num[:, :, :, 0].reshape(bsz, dil, l, h, dh).transpose(0, 2, 1, 3, 4).reshape(bsz, s, h, dh))
        ms.append(m[..., 0].reshape(bsz, dil, l, h).transpose(0, 2, 1, 3).reshape(bsz, s, h))
        dens.append(den[..., 0].reshape(bsz, dil, l, h).transpose(0, 2, 1, 3).reshape(bsz, s, h))
    m_tot = ms[0]
    for m in ms[1:]:
        m_tot = jnp.maximum(m_tot, m)
    num_tot = sum(nm * jnp.exp(m - m_tot)[..., None] for nm, m in zip(nums, ms))
    den_tot = sum(dn * jnp.exp(m - m_tot) for dn, m in zip(dens, ms))
    return (num_tot / den_tot[..., None]).astype(q.dtype)

def sliding_window_sink_attention(q, k, v, sink):
    bsz, s, hq, dh = q.shape
    hk = k.shape[2]
    g = hq // hk
    num, m, den = banded_partial(q.reshape(bsz, s, hk, g, dh), k, v, SWA_WINDOW - 1)
    sink_g = sink.astype(jnp.float32).reshape(hk, g)
    m2 = jnp.maximum(m, sink_g)
    w = jnp.exp(m - m2)
    out = num * w[..., None] / (den * w + jnp.exp(sink_g - m2))[..., None]
    return out.reshape(bsz, s, hq, dh).astype(q.dtype)

def mixer_rglru_fox(h, w_in, conv_w, conv_b, w_a, b_a, w_i, b_i, lam, b_f, w_out):
    bsz, s, _ = h.shape
    z = h @ w_in
    u, gate, q, k, v, f_logit = jnp.split(
        z, [LRU_WIDTH, 2 * LRU_WIDTH, 2 * LRU_WIDTH + FOX_W, 2 * LRU_WIDTH + 2 * FOX_W, 2 * LRU_WIDTH + 3 * FOX_W], axis=-1)
    y_a = rg_lru(causal_depthwise_conv(u, conv_w, conv_b), w_a, b_a, w_i, b_i, lam) * jax.nn.gelu(gate)
    log_f = jax.nn.log_sigmoid(f_logit.astype(jnp.float32) + b_f.astype(jnp.float32))
    shp = (bsz, s, FOX_HEADS, HEAD_DIM)
    y_b = forgetting_attention(q.reshape(shp), k.reshape(shp), v.reshape(shp), log_f).reshape(bsz, s, FOX_W)
    return jnp.concatenate([y_a, y_b], axis=-1) @ w_out

def mixer_dilated_swa(h, w_in, sink, w_out):
    bsz, s, _ = h.shape
    pos = jnp.arange(s)
    z = h @ w_in
    qc, kc, vc, qd, kd, vd = jnp.split(
        z, [DIL_W, 2 * DIL_W, 3 * DIL_W, 3 * DIL_W + SWA_QW, 3 * DIL_W + SWA_QW + SWA_KW], axis=-1)
    dshp = (bsz, s, DIL_HEADS, HEAD_DIM)
    y_c = dilated_attention(rope(qc.reshape(dshp), pos), rope(kc.reshape(dshp), pos), vc.reshape(dshp))
    kshp = (bsz, s, SWA_KV_HEADS, HEAD_DIM)
    y_d = sliding_window_sink_attention(rope(qd.reshape(bsz, s, SWA_Q_HEADS, HEAD_DIM), pos),
                                        rope(kd.reshape(kshp), pos), vd.reshape(kshp), sink)
    return jnp.concatenate([y_c.reshape(bsz, s, DIL_W), y_d.reshape(bsz, s, SWA_QW)], axis=-1) @ w_out

def memory_cross_attention(h, mem, g_mem, w_q, w_kv, w_o):
    bsz, s, _ = h.shape
    mem_n = rmsnorm(mem, g_mem)
    q = (h @ w_q).reshape(bsz, s, XA_HEADS, XA_HEAD_DIM)
    k, v = jnp.split(mem_n @ w_kv, 2, axis=-1)
    k = k.reshape(bsz, -1, XA_HEADS, XA_HEAD_DIM)
    v = v.reshape(bsz, -1, XA_HEADS, XA_HEAD_DIM)
    sc = jnp.einsum("bqhd,bkhd->bhqk", q, k).astype(jnp.float32) * XA_HEAD_DIM ** -0.5
    p = jax.nn.softmax(sc, axis=-1)
    o = jnp.einsum("bhqk,bkhd->bqhd", p, v.astype(jnp.float32)).astype(h.dtype)
    return o.reshape(bsz, s, D_MODEL) @ w_o

def squared_relu_mlp(h, w_up, w_down):
    return jnp.square(jax.nn.relu(h @ w_up)) @ w_down

def first_inputs(seed: int = 0) -> dict:
    key = jax.random.key(seed)
    ks = iter(jax.random.split(key, 40))
    f32 = jnp.float32

    def nrm(shape, scale):
        return scale * jax.random.normal(next(ks), shape, f32)

    def gain(shape):
        return 1.0 + 0.05 * jax.random.normal(next(ks), shape, f32)

    a8 = jax.random.uniform(next(ks), (N_EVEN, LRU_WIDTH), f32, 0.9, 0.999)
    a0 = a8 ** (1.0 / LRU_C)
    lru_lambda = jnp.log(a0) - jnp.log1p(-a0)
    return {
        "x": nrm((BATCH, SEQ, D_MODEL), 1.0),
        "mem": nrm((BATCH, MEM_LEN, D_MODEL), 1.0),
        "ab_norm": gain((N_EVEN, D_MODEL)),
        "ab_w_in": nrm((N_EVEN, D_MODEL, AB_IN), D_MODEL ** -0.5),
        "ab_conv_w": nrm((N_EVEN, CONV_WIDTH, LRU_WIDTH), CONV_WIDTH ** -0.5),
        "ab_conv_b": nrm((N_EVEN, LRU_WIDTH), 0.05),
        "lru_w_a": nrm((N_EVEN, LRU_BLOCKS, LRU_BLOCK, LRU_BLOCK), LRU_BLOCK ** -0.5),
        "lru_b_a": nrm((N_EVEN, LRU_WIDTH), 0.05),
        "lru_w_i": nrm((N_EVEN, LRU_BLOCKS, LRU_BLOCK, LRU_BLOCK), LRU_BLOCK ** -0.5),
        "lru_b_i": nrm((N_EVEN, LRU_WIDTH), 0.05),
        "lru_lambda": lru_lambda,
        "fox_b_f": jax.random.uniform(next(ks), (N_EVEN, FOX_HEADS), f32, 1.0, 4.0),
        "ab_w_out": nrm((N_EVEN, AB_MIX, D_MODEL), AB_MIX ** -0.5),
        "cd_norm": gain((N_ODD, D_MODEL)),
        "cd_w_in": nrm((N_ODD, D_MODEL, CD_IN), D_MODEL ** -0.5),
        "cd_sink": nrm((N_ODD, SWA_Q_HEADS), 0.5),
        "cd_w_out": nrm((N_ODD, CD_MIX, D_MODEL), CD_MIX ** -0.5),
        "xa_norm": gain((DEPTH, D_MODEL)),
        "xa_mem_norm": gain((DEPTH, D_MODEL)),
        "xa_w_q": nrm((DEPTH, D_MODEL, D_MODEL), D_MODEL ** -0.5),
        "xa_w_kv": nrm((DEPTH, D_MODEL, 2 * D_MODEL), D_MODEL ** -0.5),
        "xa_w_o": nrm((DEPTH, D_MODEL, D_MODEL), D_MODEL ** -0.5),
        "mlp_norm": gain((DEPTH, D_MODEL)),
        "mlp_w_up": nrm((DEPTH, D_MODEL, D_FF), D_MODEL ** -0.5),
        "mlp_w_down": nrm((DEPTH, D_FF, D_MODEL), D_FF ** -0.5),
        "final_norm": gain((D_MODEL,)),
    }

def first_block(x, mem, ab_norm, ab_w_in, ab_conv_w, ab_conv_b, lru_w_a, lru_b_a, lru_w_i, lru_b_i,
              lru_lambda, fox_b_f, ab_w_out, cd_norm, cd_w_in, cd_sink, cd_w_out,
              xa_norm, xa_mem_norm, xa_w_q, xa_w_kv, xa_w_o, mlp_norm, mlp_w_up, mlp_w_down, final_norm):
    h = x
    for layer in range(DEPTH):
        j = layer // 2
        if layer % 2 == 0:
            h = h + mixer_rglru_fox(rmsnorm(h, ab_norm[j]), ab_w_in[j], ab_conv_w[j], ab_conv_b[j],
                                    lru_w_a[j], lru_b_a[j], lru_w_i[j], lru_b_i[j], lru_lambda[j],
                                    fox_b_f[j], ab_w_out[j])
        else:
            h = h + mixer_dilated_swa(rmsnorm(h, cd_norm[j]), cd_w_in[j], cd_sink[j], cd_w_out[j])
        h = h + memory_cross_attention(rmsnorm(h, xa_norm[layer]), mem, xa_mem_norm[layer],
                                       xa_w_q[layer], xa_w_kv[layer], xa_w_o[layer])
        h = h + squared_relu_mlp(rmsnorm(h, mlp_norm[layer]), mlp_w_up[layer], mlp_w_down[layer])
    return rmsnorm(h, final_norm)


DEPTH_2 = 1

GRID_W = 64
N_Q_HEADS = 8
N_KV_HEADS = 2
ATTN_WIDTH = N_Q_HEADS * HEAD_DIM
KV_WIDTH = N_KV_HEADS * HEAD_DIM
Q_BLOCK = 128
DN_HEADS = 8
DN_HEAD_DIM = 64
DN_WIDTH = DN_HEADS * DN_HEAD_DIM
CONV_WIDTH_2 = 5
CHUNK = 64
N_BRANCHES = 2
N_EXPERTS = 16
CAPACITY_FACTOR = 2
D_EXPERT = 1024
IN_SPLITS = (ATTN_WIDTH, KV_WIDTH, KV_WIDTH, DN_WIDTH, DN_WIDTH, DN_WIDTH, DN_WIDTH, 2 * DN_HEADS, 2 * DN_HEADS, N_BRANCHES * D_MODEL)
D_IN = sum(IN_SPLITS)


def rmsnorm_2(x, w):
    xf = x.astype(jnp.float32)
    y = xf * lax.rsqrt(jnp.mean(xf * xf, axis=-1, keepdims=True) + EPS)
    return (y * w.astype(jnp.float32)).astype(x.dtype)

def l2norm(x):
    xf = x.astype(jnp.float32)
    return xf * lax.rsqrt(jnp.sum(xf * xf, axis=-1, keepdims=True) + EPS)

def heads(t, n):
    B, S, _ = t.shape
    return t.reshape(B, S, n, -1).transpose(0, 2, 1, 3)

def rope_axis(x, pos):
    d = x.shape[-1]
    freqs = ROPE_THETA ** (-(jnp.arange(d // 2, dtype=jnp.float32) * 2.0 / d))
    ang = pos.astype(jnp.float32)[:, None] * freqs[None, :]
    cos = jnp.concatenate([jnp.cos(ang), jnp.cos(ang)], axis=-1)
    sin = jnp.concatenate([jnp.sin(ang), jnp.sin(ang)], axis=-1)
    xf = x.astype(jnp.float32)
    x1, x2 = xf[..., : d // 2], xf[..., d // 2 :]
    rot = jnp.concatenate([-x2, x1], axis=-1)
    return (xf * cos + rot * sin).astype(x.dtype)

def axial_rope(x, row, col):
    hd = x.shape[-1] // 2
    return jnp.concatenate([rope_axis(x[..., :hd], row), rope_axis(x[..., hd:], col)], axis=-1)

def block_attention(q, k, v):
    B, Hq, S, dh = q.shape
    Hkv = k.shape[1]
    G = Hq // Hkv
    nb = S // Q_BLOCK
    qb = q.reshape(B, Hkv, G, nb, Q_BLOCK, dh).transpose(3, 0, 1, 2, 4, 5).astype(jnp.float32)
    kf = k.astype(jnp.float32)
    vf = v.astype(jnp.float32)
    scale = dh ** -0.5

    def one_block(qi):
        s = jnp.einsum('bhgqd,bhkd->bhgqk', qi, kf) * scale
        p = jax.nn.softmax(s, axis=-1)
        return jnp.einsum('bhgqk,bhkd->bhgqd', p, vf)

    o = lax.map(one_block, qb)
    return o.transpose(1, 2, 3, 0, 4, 5).reshape(B, Hq, S, dh).astype(q.dtype)

def short_conv(x, w):
    K, C = w.shape
    return lax.conv_general_dilated(x, w[:, None, :], window_strides=(1,), padding=[(K // 2, K // 2)],
                                    dimension_numbers=('NWC', 'WIO', 'NWC'), feature_group_count=C)

def gated_delta_chunked(q, k, v, beta, g):
    B, H, S, dk = q.shape
    dv = v.shape[-1]
    N = S // CHUNK
    q = q.reshape(B, H, N, CHUNK, dk)
    k = k.reshape(B, H, N, CHUNK, dk)
    v = v.reshape(B, H, N, CHUNK, dv)
    beta = beta.reshape(B, H, N, CHUNK)
    gc = jnp.cumsum(g.reshape(B, H, N, CHUNK), axis=-1)
    idx = jnp.arange(CHUNK)
    incl = idx[:, None] >= idx[None, :]
    strict = idx[:, None] > idx[None, :]
    decay = jnp.exp(jnp.where(incl, gc[..., :, None] - gc[..., None, :], -jnp.inf))
    kb = k * beta[..., None]
    vb = v * beta[..., None]
    L = jnp.where(strict, jnp.einsum('bhncd,bhnsd->bhncs', kb, k) * decay, 0.0)
    eye = jnp.eye(CHUNK, dtype=jnp.float32)
    T = lax.linalg.triangular_solve(eye + L, jnp.broadcast_to(eye, L.shape), left_side=True, lower=True,
                                    unit_diagonal=True)
    u = T @ vb
    w = T @ (kb * jnp.exp(gc)[..., None])
    a_intra = jnp.where(incl, jnp.einsum('bhncd,bhnsd->bhncs', q, k) * decay, 0.0)
    qg = q * jnp.exp(gc)[..., None]
    kd = k * jnp.exp(gc[..., -1:] - gc)[..., None]
    gl = jnp.exp(gc[..., -1])
    xs = tuple(jnp.moveaxis(t, 2, 0) for t in (u, w, a_intra, qg, kd, gl))

    def step(state, inp):
        u_n, w_n, a_n, qg_n, kd_n, gl_n = inp
        v_new = u_n - w_n @ state
        o_n = qg_n @ state + a_n @ v_new
        state = state * gl_n[..., None, None] + jnp.einsum('bhck,bhcv->bhkv', kd_n, v_new)
        return state, o_n

    _, o = lax.scan(step, jnp.zeros((B, H, dk, dv), jnp.float32), xs)
    return jnp.moveaxis(o, 0, 2).reshape(B, H, S, dv)

def hybrid_mixer(h, row, col, w_in, q_norm_w, k_norm_w, conv_w, a_log, dt_bias, dn_norm_w, w_attn_up, w_dn_up, w_o):
    B, S, D = h.shape
    proj = h @ w_in
    aq, ak, av, dq, dk, dv, dz, b_raw, a_raw, g_raw = jnp.split(proj, np.cumsum(IN_SPLITS)[:-1].tolist(), axis=-1)

    q = axial_rope(rmsnorm_2(heads(aq, N_Q_HEADS), q_norm_w), row, col)
    k = axial_rope(rmsnorm_2(heads(ak, N_KV_HEADS), k_norm_w), row, col)
    v = heads(av, N_KV_HEADS)
    attn = block_attention(q, k, v).transpose(0, 2, 1, 3).reshape(B, S, ATTN_WIDTH)

    qkv = jax.nn.silu(short_conv(jnp.concatenate([dq, dk, dv], axis=-1), conv_w))
    cq, ck, cv = jnp.split(qkv, 3, axis=-1)
    qd = l2norm(heads(cq, DN_HEADS)) * (DN_HEAD_DIM ** -0.5)
    kd = l2norm(heads(ck, DN_HEADS))
    vd = heads(cv, DN_HEADS).astype(jnp.float32)
    beta = jax.nn.sigmoid(b_raw.astype(jnp.float32)).reshape(B, S, 2, DN_HEADS).transpose(2, 0, 3, 1)
    a_in = a_raw.astype(jnp.float32).reshape(B, S, 2, DN_HEADS) + dt_bias.astype(jnp.float32)
    g = -jnp.exp(a_log.astype(jnp.float32))[:, None, :, None] * jax.nn.softplus(a_in.transpose(2, 0, 3, 1))
    flip = lambda t: jnp.flip(t, axis=2)
    o_fwd = gated_delta_chunked(qd, kd, vd, beta[0], g[0])
    o_bwd = flip(gated_delta_chunked(flip(qd), flip(kd), flip(vd), flip(beta[1]), flip(g[1])))
    o = (o_fwd + o_bwd).transpose(0, 2, 1, 3)
    o = rmsnorm_2(o, dn_norm_w) * jax.nn.silu(dz.astype(jnp.float32).reshape(B, S, DN_HEADS, DN_HEAD_DIM))
    dn = o.reshape(B, S, DN_WIDTH).astype(h.dtype)

    gate_a, gate_d = jnp.split(jax.nn.sigmoid(g_raw), N_BRANCHES, axis=-1)
    merged = gate_a * (attn @ w_attn_up) + gate_d * (dn @ w_dn_up)
    return merged @ w_o

def expert_choice_ffn(h, w_router, w_gate, w_up, w_down):
    B, S, D = h.shape
    cap = CAPACITY_FACTOR * S // N_EXPERTS
    aff = jax.nn.softmax((h @ w_router).astype(jnp.float32), axis=-1)
    gates, idx = lax.top_k(aff.transpose(0, 2, 1), cap)
    bidx = jnp.arange(B)[:, None, None]
    xe = h[bidx, idx]
    hg = jnp.einsum('becd,edf->becf', xe, w_gate)
    hu = jnp.einsum('becd,edf->becf', xe, w_up)
    y = jnp.einsum('becf,efd->becd', jax.nn.silu(hg) * hu, w_down)
    y = y * gates[..., None].astype(y.dtype)
    return jnp.zeros_like(h).at[bidx, idx].add(y)

def second_inputs(seed: int = 0) -> dict:
    key = jax.random.key(seed)
    ks = jax.random.split(key, 24)
    f32 = jnp.float32

    def nrm(k, shape, fan_in):
        return jax.random.normal(k, shape, f32) * (fan_in ** -0.5)

    def gain(k, shape):
        return 1.0 + 0.02 * jax.random.normal(k, shape, f32)

    dt = jnp.exp(jax.random.uniform(ks[11], (DEPTH_2, 2, DN_HEADS), f32, np.log(1e-3), np.log(1e-1)))
    return {
        'x': jax.random.normal(ks[0], (BATCH, SEQ, D_MODEL), f32),
        'c': jax.random.normal(ks[1], (BATCH, D_MODEL), f32),
        'w_ada': nrm(ks[2], (DEPTH_2, D_MODEL, 6 * D_MODEL), D_MODEL),
        'b_ada': 0.01 * jax.random.normal(ks[3], (DEPTH_2, 6 * D_MODEL), f32),
        'norm1_w': gain(ks[4], (DEPTH_2, D_MODEL)),
        'w_in': nrm(ks[5], (DEPTH_2, D_MODEL, D_IN), D_MODEL),
        'q_norm_w': gain(ks[6], (DEPTH_2, HEAD_DIM)),
        'k_norm_w': gain(ks[7], (DEPTH_2, HEAD_DIM)),
        'conv_w': nrm(ks[8], (DEPTH_2, CONV_WIDTH_2, 3 * DN_WIDTH), CONV_WIDTH_2),
        'a_log': jnp.log(jax.random.uniform(ks[9], (DEPTH_2, 2, DN_HEADS), f32, 1.0, 16.0)),
        'dt_bias': dt + jnp.log(-jnp.expm1(-dt)),
        'dn_norm_w': gain(ks[10], (DEPTH_2, DN_HEAD_DIM)),
        'w_attn_up': nrm(ks[12], (DEPTH_2, ATTN_WIDTH, D_MODEL), ATTN_WIDTH),
        'w_dn_up': nrm(ks[13], (DEPTH_2, DN_WIDTH, D_MODEL), DN_WIDTH),
        'w_o': nrm(ks[14], (DEPTH_2, D_MODEL, D_MODEL), D_MODEL),
        'norm2_w': gain(ks[15], (DEPTH_2, D_MODEL)),
        'w_router': nrm(ks[16], (DEPTH_2, D_MODEL, N_EXPERTS), D_MODEL),
        'w_gate': nrm(ks[17], (DEPTH_2, N_EXPERTS, D_MODEL, D_EXPERT), D_MODEL),
        'w_up': nrm(ks[18], (DEPTH_2, N_EXPERTS, D_MODEL, D_EXPERT), D_MODEL),
        'w_down': nrm(ks[19], (DEPTH_2, N_EXPERTS, D_EXPERT, D_MODEL), D_EXPERT),
    }

def second_block(x, c, w_ada, b_ada, norm1_w, w_in, q_norm_w, k_norm_w, conv_w, a_log, dt_bias, dn_norm_w,
              w_attn_up, w_dn_up, w_o, norm2_w, w_router, w_gate, w_up, w_down):
    B, S, D = x.shape
    rows = S // GRID_W
    row = jnp.broadcast_to(jnp.arange(rows)[:, None], (rows, GRID_W)).reshape(S)
    col = jnp.broadcast_to(jnp.arange(GRID_W)[None, :], (rows, GRID_W)).reshape(S)
    for l in range(DEPTH_2):
        mod = jax.nn.silu(c) @ w_ada[l] + b_ada[l]
        sh1, sc1, gt1, sh2, sc2, gt2 = [m[:, None, :] for m in jnp.split(mod, 6, axis=-1)]
        h = rmsnorm_2(x, norm1_w[l]) * (1.0 + sc1) + sh1
        x = x + gt1 * hybrid_mixer(h, row, col, w_in[l], q_norm_w[l], k_norm_w[l], conv_w[l], a_log[l], dt_bias[l],
                                   dn_norm_w[l], w_attn_up[l], w_dn_up[l], w_o[l])
        h2 = rmsnorm_2(x, norm2_w[l]) * (1.0 + sc2) + sh2
        x = x + gt2 * expert_choice_ffn(h2, w_router[l], w_gate[l], w_up[l], w_down[l])
    return x


def setup_inputs(seed=0):
    out = dict(first_inputs(seed))
    for name, value in second_inputs(seed + 1).items():
        if name != "x":
            out[name + "_2"] = value
    return out


def reference(
    x, mem, ab_norm, ab_w_in, ab_conv_w, ab_conv_b, lru_w_a, lru_b_a, lru_w_i, lru_b_i,
    lru_lambda, fox_b_f, ab_w_out, cd_norm, cd_w_in, cd_sink, cd_w_out, xa_norm, xa_mem_norm,
    xa_w_q, xa_w_kv, xa_w_o, mlp_norm, mlp_w_up, mlp_w_down, final_norm, c_2, w_ada_2, b_ada_2,
    norm1_w_2, w_in_2, q_norm_w_2, k_norm_w_2, conv_w_2, a_log_2, dt_bias_2, dn_norm_w_2,
    w_attn_up_2, w_dn_up_2, w_o_2, norm2_w_2, w_router_2, w_gate_2, w_up_2, w_down_2,
):
    x = first_block(
        x, mem, ab_norm, ab_w_in, ab_conv_w, ab_conv_b, lru_w_a, lru_b_a, lru_w_i, lru_b_i,
        lru_lambda, fox_b_f, ab_w_out, cd_norm, cd_w_in, cd_sink, cd_w_out, xa_norm,
        xa_mem_norm, xa_w_q, xa_w_kv, xa_w_o, mlp_norm, mlp_w_up, mlp_w_down, final_norm,
    )
    return second_block(
        x, c_2, w_ada_2, b_ada_2, norm1_w_2, w_in_2, q_norm_w_2, k_norm_w_2, conv_w_2, a_log_2,
        dt_bias_2, dn_norm_w_2, w_attn_up_2, w_dn_up_2, w_o_2, norm2_w_2, w_router_2, w_gate_2,
        w_up_2, w_down_2,
    )


_drawn_inputs = setup_inputs


def setup_inputs(seed=0):
    import zlib

    import numpy as np

    out = dict(_drawn_inputs(seed))
    spreads = {}
    factors = {'lru_b_a': 8.0,
     'lru_b_i': 3.425,
     'cd_sink': 8.0,
     'xa_norm': 3.073,
     'b_ada_2': 5.005,
     'norm1_w_2': 3.358,
     'q_norm_w_2': 8.0,
     'k_norm_w_2': 8.0,
     'dn_norm_w_2': 7.719,
     'norm2_w_2': 3.332}
    for name, (base, spread) in spreads.items():
        noise = np.random.default_rng([zlib.crc32(name.encode()), seed]).standard_normal(out[name].shape)
        drawn = base * np.exp(spread * noise) if base else spread * noise
        out[name] = __import__('jax').numpy.asarray(drawn.astype(out[name].dtype))
    for name, factor in factors.items():
        out[name] = (out[name] * factor).astype(out[name].dtype)
    return out
```

```python
import math
from contextlib import ExitStack

import numpy as np
import concourse.bass as bass
from concourse import mybir

F32 = mybir.dt.float32
ALU = mybir.AluOpType
ACT = mybir.ActivationFunctionType
AX = mybir.AxisListType

P = 128
S = 256
D = 1024
DC = D // P
TT = S // P
FF = 4096
FC = FF // P
HD = 64
NE = 16
CAP = 2 * S // NE
EG = P // CAP
EPS = 1e-6
NEG = -1.0e30
SLOTS = 6
UNIT = DC * 512
NLEV = 7

COLS = {}
NCOL = 0
for _name, _n in (("ab_norm", 8), ("cd_norm", 8), ("xa_norm0", 8), ("xa_norm1", 8),
                  ("mem_norm0", 8), ("mem_norm1", 8), ("mlp_norm0", 8), ("mlp_norm1", 8),
                  ("final_norm", 8), ("norm1", 8), ("norm2", 8), ("conv_w", 16), ("conv_b", 4),
                  ("b_a", 4), ("b_i", 4), ("lam", 4), ("c", 8), ("b_ada", 48),
                  ("conv2_w", 60), ("q_norm", 1), ("k_norm", 1), ("dn_norm", 1),
                  ("fox_b", 1), ("sink", 8), ("a_log", 16), ("dt_bias", 16)):
    COLS[_name] = (NCOL, _n)
    NCOL += _n

CONS = {}
NCON = 0
for _name, _n in (("ident", P), ("ones", P), ("blk", P), ("rot1", P), ("rot2", P),
                  ("cum", 2 * P), ("cos1", S), ("sin1", S), ("cos2", S), ("sin2", S),
                  ("m_fox", 2 * S), ("m_dil", 2 * S), ("m_swa", 2 * S), ("neg", 2 * P),
                  ("lev", NLEV * 2 * P), ("slot", CAP), ("eps", 1)):
    CONS[_name] = (NCON, _n)
    NCON += _n


def constants():
    c = np.zeros((P, NCON), np.float32)

    def put(name, a):
        at, n = CONS[name]
        a = np.asarray(a, np.float32).reshape(a.shape[0], -1)
        c[:a.shape[0], at:at + n] = a

    i = np.arange(P)
    put("ident", np.eye(P))
    put("ones", np.ones((P, P)))
    put("blk", (i[:, None] // HD == i[None, :] // HD))

    def rotation(width):
        m = np.zeros((P, P))
        h = width // 2
        for o in range(P):
            if o % width < h:
                m[o + h, o] = -1.0
            else:
                m[o - h, o] = 1.0
        return m

    put("rot1", rotation(64))
    put("rot2", rotation(32))
    s, t = i[:, None], i[None, :]
    put("cum", np.stack([s <= t, s >= t], 1))
    pos = np.arange(S, dtype=np.float32)
    inv = np.float32(10000.0) ** (-np.arange(32, dtype=np.float32) / np.float32(32))
    ang = pos[None, :] * inv[i % 32][:, None]
    put("cos1", np.cos(ang))
    put("sin1", np.sin(ang))
    fr = np.float32(10000.0) ** (-(np.arange(16, dtype=np.float32) * np.float32(2.0) / np.float32(32)))
    where = np.where((i % 64 < 32)[:, None], np.floor(pos / 64)[None, :], (pos % 64)[None, :]).astype(np.float32)
    ang = where * fr[i % 16][:, None]
    put("cos2", np.cos(ang))
    put("sin2", np.sin(ang))
    q = np.arange(S)[:, None]
    k = np.arange(S)[None, :]
    d = q - k

    def blocks(m):
        return m.reshape(2, P, S).transpose(1, 0, 2)

    put("m_fox", blocks(np.where(d >= 0, 0.0, NEG)))
    times = ((d >= 0) & (d <= 128)).astype(int) + ((d >= 0) & (d % 4 == 0)) + ((d >= 0) & (d % 16 == 0))
    put("m_dil", blocks(np.where(times > 0, np.log(np.maximum(times, 1)), NEG)))
    put("m_swa", blocks(np.where((d >= 0) & (d <= 127), 0.0, NEG)))
    put("neg", np.stack([np.where(s <= t, 0.0, NEG), np.where(s >= t, 0.0, NEG)], 1))
    lev = np.zeros((P, NLEV, 2, P))
    for n in range(NLEV):
        w = 1 << n
        low = (s // (2 * w) == t // (2 * w)) & (s // w % 2 == 0) & (t // w % 2 == 1)
        lev[:, n, 0] = low
        lev[:, n, 1] = low.T
    put("lev", lev)
    put("slot", np.broadcast_to(np.arange(CAP), (P, CAP)))
    put("eps", np.full((P, 1), EPS))
    return c


def program(nc, a, out):
    ctx = ExitStack()
    with ctx:
        def sb(name, n):
            return ctx.enter_context(nc.sbuf_tensor(name, [P, n], F32))

        def sem(name):
            return ctx.enter_context(nc.semaphore(name))

        ring = sb("ring", SLOTS * UNIT)
        xTt, hTt, side = sb("xT", DC * S), sb("hT", DC * S), sb("side", 2080)
        cols, cons, small_w = sb("cols", NCOL), sb("cons", NCON), sb("small_w", 64 + 256 + 128)
        arena, lru_w_, rtp = sb("arena", 11312), sb("lru_w", 1024), sb("root_pairs", 1024)
        more, rt, rs, sml = sb("more", 1280), sb("root", S), sb("rstd", S), sb("sml", 760)
        pb = ctx.enter_context(nc.psum_tensor("pb", [P, 8, 512], F32))

        def view(t, at, *shape):
            v = t[:, at:at + math.prod(shape)]
            if len(shape) == 2:
                return v.rearrange("p (a b) -> p a b", a=shape[0])
            if len(shape) == 3:
                return v.rearrange("p (a b c) -> p a b c", a=shape[0], b=shape[1])
            return v

        def col(name, i=0, n=1):
            at = COLS[name][0] + i
            return cols[:, at:at + n]

        def con(name, *shape):
            return view(cons, CONS[name][0], *(shape or (CONS[name][1],)))

        ident, ones, blk, eps = con("ident"), con("ones"), con("blk"), con("eps")
        cum, neg = con("cum", 2, P), con("neg", 2, P)
        lev = con("lev", NLEV, 2, P)
        w_f, w_ba, w_rt = view(small_w, 0, DC, 8), view(small_w, 64, DC, 32), view(small_w, 320, DC, NE)

        xT, hT, memT = view(xTt, 0, DC, S), view(hTt, 0, DC, S), view(side, 0, DC, S)
        qT, kT, vt, yT = (view(arena, 2048 * i, *((2, 1024) if i == 2 else (DC, S))) for i in range(4))
        sm, pr, pT = view(arena, 8192, 2, 2, S), view(arena, 9216, 2, 2, S), view(arena, 10240, 2, 512)
        sq = view(arena, 8192, DC, S)
        mn = yT
        up, uc = view(side, 0, 4, 259), view(side, 1040, 4, S)
        gt = view(arena, 6144, 4, S)
        lru_w = view(lru_w_, 0, 8, P)
        l_r, l_i, l_a = view(side, 0, 4, S), view(hTt, 0, 4, S), view(hTt, 1024, 4, S)
        l_g = view(lru_w_, 0, 4, S)
        fz = [arena[0:8, 1024 + S * i:1024 + S * (i + 1)] for i in range(4)]
        fy = [arena[0:8, 3072 + S * i:3072 + S * (i + 1)] for i in range(4)]
        cc = fy[3]
        zr, ra, rb = view(arena, 6144, 14, S), view(arena, 9728, 2, S), view(arena, 10240, 2, S)
        hid, hrelu = view(arena, 0, FC, S), view(arena, 10240, 2, 512)
        cv, cp = view(arena, 0, 12, S), view(arena, 8192, 12, 260)
        dz = view(arena, 6144, 4, S)
        tA, tB = view(arena, 7168, 4, S), view(arena, 8192, 4, S)
        cth, dzt = view(arena, 5120, 4, S), view(more, 0, 4, S)
        gq, gk, gv = view(side, 0, 4, S), view(arena, 3072, 2, S), view(arena, 3584, 2, P)
        ra2, rb2 = view(arena, 4096, 2, S), view(arena, 4608, 2, S)
        gaT, d_o = view(side, 1024, 4, S), view(side, 0, 4, S)
        ktok, vtok = view(arena, 9216, 2, 512), view(arena, 10240, 2, 512)
        d_LT = [view(arena, 3072, 4, P), view(arena, 3584, 4, P)]
        d_AT = [view(arena, 4096, 4, P), view(arena, 4608, 4, P)]
        d_T = [view(arena, 5120, 4, P), view(arena, 5632, 4, P)]
        d_TT = [view(arena, 8192, 4, P), view(arena, 8704, 4, P)]
        d_X = [view(lru_w_, 0, 4, P), view(lru_w_, 512, 4, P)]
        d_LM = [view(rtp, 0, 4, P), view(rtp, 512, 4, P)]
        d_kg = [view(arena, 7168, 2, P), view(arena, 7424, 2, P)]
        d_qg = [view(arena, 7680, 2, P), view(arena, 7936, 2, P)]
        d_vn = [view(more, 0, 4, HD), view(more, 256, 4, HD)]
        d_v2 = [view(more, 512, 2, HD), view(more, 640, 2, HD)]
        d_S = [view(more, 768, 2, HD), view(more, 896, 2, HD)]
        d_kd = [view(more, 1024, 2, HD), view(more, 1152, 2, HD)]
        dnT = view(arena, 3072, 4, S)
        sga, sgd = view(arena, 8192, DC, S), view(arena, 0, DC, S)
        h2t, xe, ye = view(arena, 0, 2, 1024), view(arena, 2048, DC, 512), view(arena, 6144, DC, 512)
        rw = [arena[0:NE, 6144 + S * i:6144 + S * (i + 1)] for i in range(4)]
        Ph, Pg, PGt = view(arena, 10240, 2, 512), view(side, 1024, 2, 512), view(side, 0, 4, S)
        xs, hg, tg = view(hTt, 0, DC, CAP), view(hTt, S, DC, CAP), view(hTt, 2 * S, DC, CAP)
        ytok = view(arena, 2048, 4, 1024)

        sat = [0]

        def small(*shape):
            v = view(sml, sat[0], *shape)
            sat[0] += math.prod(shape)
            return v

        hba, hbi, c4 = small(4), small(4), small(4)
        sp_t = [small(4) for _ in range(4)]
        nmx, den, es, mxr = small(2, 2), small(2, 2), small(2, 2), small(2, 2)
        csil, modc, g1s, g2s, wq8, hgt1 = small(8), small(48), small(8), small(8), small(1), small(8)
        beta, gl, gct, ekd = small(2, NE), small(2, NE), small(2, NE), small(2, NE)
        sp_a = [small(2, NE) for _ in range(4)]
        alog = small(NE)
        aff, selc, raff = small(2, NE), small(2, NE), small(2)
        top8 = small(8)

        units = []

        def unit(w, r0, nr, c0, ncol):
            units.append((w, r0, nr, c0, ncol))

        def matrix(w, n=D, c0=0):
            for c in range(c0, c0 + n, 512):
                unit(w, 0, D, c, min(512, c0 + n - c))

        matrix(a["ab_w_in"], 2560)
        matrix(a["ab_w_out"])
        for layer in range(2):
            if layer:
                matrix(a["cd_w_in"], 2048)
                unit(a["cd_w_kv"], 0, D, 0, 384)
                matrix(a["cd_w_out"])
            matrix(a["xa_w_kv"][layer], 2 * D)
            matrix(a["xa_w_q"][layer])
            matrix(a["xa_w_o"][layer])
            matrix(a["mlp_w_up"][layer], FF)
            for c in range(0, D, 512):
                for r in range(0, FF, D):
                    unit(a["mlp_w_down"][layer], r, D, c, 512)
        matrix(a["w_ada_2"], 6 * D)
        for c0 in (768, 1280, 1792, 0):
            unit(a["w_in_2"], 0, D, c0, 512)
        unit(a["w_kv_2"], 0, D, 0, 384)
        for c0 in (2304, 2848, 3360, 3872, 4384):
            unit(a["w_in_2"], 0, D, c0, 512)
        unit(a["w_attn_up_2"], 0, 512, 0, D)
        unit(a["w_dn_up_2"], 0, 512, 0, D)
        matrix(a["w_o_2"])
        NDENSE = len(units)

        def slot_ap(u):
            w, r0, nr, c0, ncol = units[u]
            at = (u % SLOTS) * UNIT
            return ring[:, at:at + (nr // P) * ncol].rearrange("p (c n) -> p c n", n=ncol)

        ESLOT = [(NDENSE + j) % SLOTS for j in range(SLOTS)]
        EBASE = [(NDENSE + j) // SLOTS for j in range(SLOTS)]

        loaded = [sem(f"slot_loaded{i}") for i in range(SLOTS)]
        filled = [sem(f"bank_filled{i}") for i in range(8)]
        freed = [sem(f"bank_freed{i}") for i in range(8)]
        small_in, x_in, mem_in, out_sent = sem("small_loaded"), sem("x_loaded"), sem("mem_loaded"), sem("out_sent")
        norm_sq, h_ready, fin_ready = sem("norm_squares"), sem("h_ready"), sem("final_normed")
        mn_ready = sem("mem_normed")
        pads, uc_ready, gin_ready, gth_ready = sem("pads_zeroed"), sem("u_convolved"), sem("gelu_inner"), sem("gelu_tanh")
        hb_ready, ly_ready, la_ready = sem("half_biases"), sem("lru_exponent"), sem("lru_decay")
        lw_ready, lx_ready, lru_out = sem("lru_ratio"), sem("lru_root"), sem("lru_out")
        sp_abs, sp_exp, f_ready = sem("softplus_abs"), sem("softplus_exp"), sem("forget_cumulated")
        rot_ready = sem("rotated")
        mx_ready, p_ready, pn_ready, pt_ready = sem("row_max"), sem("probs_raw"), sem("probs_scaled"), sem("probs_turned")
        hid_ready = sem("mlp_squared")
        c_tanh, c_ready, mod_ready = sem("c_tanh"), sem("c_silu"), sem("modulation")
        cin_ready, cv_ready, cvt_ready, cvs_ready = sem("conv_in"), sem("convolved"), sem("conv_tanh"), sem("conv_silu")
        l2_sq, l2_ready = sem("head_squares"), sem("head_normed")
        ba_th, g_ready, gc_ready, gx_ready = sem("beta_tanh"), sem("log_decay"), sem("cumulated"), sem("decay_rate")
        dd_ready, dec_ready, er_ready = sem("decay_diff"), sem("decay_exp"), sem("decay_row_exp")
        LT_ready, LM_ready, TT_ready = sem("triangle"), sem("level_masked"), sem("first_level")
        kg_ready, kd_ready, ekd_ready, ekx_ready = sem("decayed_kq"), sem("decayed_k_rows"), sem("tile_decay"), sem("tile_exp")
        dn_ready, dzt_ready = sem("delta_gated"), sem("dz_tanh")
        mg_ready = sem("merged")
        rt_mx, rt_e, aff_ready = sem("router_max"), sem("router_exp"), sem("affinity")
        sel_ready, P_ready, PG_ready = sem("selection"), sem("one_hot"), sem("one_hot_gated")
        xs_ready, eth_ready, eg_ready, hg_ready, ye_ready = sem("expert_slice"), sem("expert_tanh"), sem("expert_gate"), sem("expert_hidden"), sem("expert_out")
        res_ready = sem("result_chunks")
        dve_step, act_step = sem("dve_step"), sem("act_step")

        block = ctx.enter_context(nc.Block())

        fillings = {}
        marks = [0] * 8
        taken = [0] * 8
        unit_read = {}

        STAGES = [("fox", 8), ("xa0", 4), ("dil", 8), ("swa", 8), ("xa1", 4), ("gqa", 8)]
        HEADS = dict(STAGES)
        FIRST_HEAD = {}
        for _s, _h in STAGES:
            FIRST_HEAD[_s] = sum(HEADS[s] for s in FIRST_HEAD)
        CAUSAL = {"fox": "m_fox", "dil": "m_dil", "swa": "m_swa"}
        WIDE = ("xa0", "xa1")
        PAIRS = [(gq[:, 0:2, :], tA[:, 0:2, :]), (gq[:, 2:4, :], tA[:, 2:4, :]), (gk, view(lru_w_, 0, 2, S))]
        DPAIRS = [(cv[:, 2 * r:2 * r + 2, :], (tA, tB)[r // 2][:, 2 * (r % 2):2 * (r % 2) + 2, :]) for r in range(4)]
        rt2 = view(rtp, 0, 2, 2, S)

        def copied(eng, *names):
            for name in names:
                b, _, use = fillings[name]
                eng.wait_ge(freed[b], use)

        def outs(stage):
            step = 1 if stage in WIDE else 2
            return [f"o{FIRST_HEAD[stage] + h}" for h in range(0, HEADS[stage], step)]

        def second(d):
            return 1 - d

        def half(h):
            return slice(HD * (h % 2), HD * (h % 2) + HD)

        @block.tensor
        def _(pe):
            at, bank, norms, hs = [0], [0], [0], [0]

            def fill(name, b=None):
                if b is None:
                    b = bank[0]
                    bank[0] = (b + 1) % 4
                if taken[b]:
                    pe.wait_ge(freed[b], taken[b])
                taken[b] += 1
                fillings[name] = (b, None, taken[b])
                return pb[:, b, :]

            def mark(ins, name, complete=True, u=None):
                b, _, use = fillings[name]
                marks[b] += 1
                ins.then_inc(filled[b], 1)
                if complete:
                    fillings[name] = (b, marks[b], use)
                if u is not None:
                    unit_read[u] = (b, marks[b])

            def take():
                u = at[0]
                at[0] += 1
                pe.wait_ge(loaded[u % SLOTS], 16 * (u // SLOTS + 1))
                return slot_ap(u), u

            def mm(o, l, r, st, sp):
                return nc.tensor.matmul(o, l, r, start=st, stop=sp)

            def chunk_wait(signal):
                base = hs[0]
                hs[0] += 8
                return lambda k: pe.wait_ge(signal, base + k + 1)

            def columns(tag, rhs, kc=DC, ready=None):
                w, u = take()
                nt = w.shape[2] // P
                for b in range(0, nt, 2):
                    ps = fill(f"{tag}{b // 2}")
                    for j in range(2):
                        for k in range(kc):
                            if ready is not None and b == 0 and j == 0:
                                ready(k)
                            last = mm(ps[:, j * S:(j + 1) * S], w[:, k, (b + j) * P:(b + j + 1) * P],
                                      rhs[:, k, :], k == 0, k == kc - 1)
                    mark(last, f"{tag}{b // 2}", u=u if b + 2 >= nt else None)

            def rows(tag, lhs, w, u, c0, n):
                for t in range(TT):
                    ps = fill(f"{tag}{t}")
                    for k in range(DC):
                        last = mm(ps[:, 0:n], lhs[:, k, t * P:(t + 1) * P], w[:, k, c0:c0 + n], k == 0, k == DC - 1)
                    mark(last, f"{tag}{t}", u=u if t == TT - 1 else None)

            def twice(tag, w):
                for g in range(2):
                    ps = fill(f"{tag}{g}")
                    for k in range(DC):
                        last = mm(ps[:, 0:S], w[:, k, g * P:(g + 1) * P], hT[:, k, :], k == 0, k == DC - 1)
                    mark(last, f"{tag}{g}")

            def norm(tag, sq=sq):
                ps = fill(f"norm_{tag}")
                for c in range(DC):
                    pe.wait_ge(norm_sq, 8 * norms[0] + c + 1)
                    last = mm(ps[:, 0:S], ones, sq[:, c, :], c == 0, c == DC - 1)
                mark(last, f"norm_{tag}")
                norms[0] += 1

            def attention(stage, ready):
                h0, heads, causal, wide = FIRST_HEAD[stage], HEADS[stage], stage in CAUSAL, stage in WIDE

                def operands(h):
                    r = half(h)
                    if wide:
                        return [(qT[:, 2 * h + j, :], kT[:, 2 * h + j, :]) for j in range(2)]
                    if stage in ("fox", "dil"):
                        return [(qT[r, h // 2, :], kT[r, h // 2, :])]
                    if stage == "swa":
                        return [(qT[r, 4 + h // 2, :], kT[r, 4 + h // 4, :])]
                    return [(gq[r, h // 2, :], gk[r, h // 4, :])]

                def values(h, kb):
                    if wide:
                        return [vt[:, kb, 256 * h + P * j:256 * h + P * (j + 1)] for j in range(2)]
                    if stage in ("fox", "dil"):
                        return [vt[:, kb, HD * h:HD * h + HD]]
                    if stage == "swa":
                        return [vt[:, kb, 512 + HD * (h // 4):512 + HD * (h // 4) + HD]]
                    return [gv[:, kb, HD * (h // 4):HD * (h // 4) + HD]]

                def scores(h):
                    n = h0 + h
                    ps = fill(f"s{n}", 4 + n % 2)
                    for qb in range(2):
                        nk = P if causal and qb == 0 else S
                        ops = operands(h)
                        o = ps[:, qb * S:qb * S + nk]
                        for j, (q, k) in enumerate(ops):
                            last = mm(o, q[:, qb * P:(qb + 1) * P], k[:, 0:nk], j == 0,
                                      j == len(ops) - 1 and stage != "fox")
                        if stage == "fox":
                            last = mm(o, ident[0:8, h:h + 1].broadcast_to([8, P]), cc[:, 0:nk], False, True)
                    mark(last, f"s{n}")

                def turn(h):
                    n = h0 + h
                    pe.wait_ge(pn_ready, n + 1)
                    ps = fill(f"t{n}", 6)
                    for kb in range(2):
                        for qb in range(2):
                            if causal and kb > qb:
                                continue
                            c = kb * S + qb * P - (P if causal and kb else 0)
                            last = nc.tensor.transpose(ps[:, c:c + P], pr[:, n % 2, qb, kb * P:(kb + 1) * P], ident)
                    mark(last, f"t{n}")

                held = [None]

                def weigh(h):
                    n = h0 + h
                    copied(pe, f"t{n}")
                    if wide or h % 2 == 0:
                        held[0] = fill(f"o{n}", 7)
                    ps = held[0]
                    for j in range(2 if wide else 1):
                        o = ps[:, j * S:(j + 1) * S] if wide else ps[half(h), 0:S]
                        mm(o, values(h, 0)[j], pT[:, n % 2, 0:S], True, False)
                        lo = P if causal else 0
                        last = mm(o[:, lo:S], values(h, 1)[j], pT[:, n % 2, S:2 * S - lo], False, True)
                    if wide or h % 2:
                        mark(last, f"o{n if wide else n - 1}")

                ready()
                scores(0)
                scores(1)
                for h in range(heads):
                    turn(h)
                    if h + 2 < heads:
                        scores(h + 2)
                    weigh(h)

            pe.wait_ge(small_in, 16 * 4)
            norm("ab")
            ready = chunk_wait(h_ready)
            for tag in ("u", "gate", "q", "k"):
                columns(f"ab_{tag}", hT, ready=ready)
                ready = None
            w, u = take()
            rows("ab_v", hT, w, u, 0, 512)
            ps = fill("ab_f")
            for k in range(DC):
                last = mm(ps[0:8, 0:S], w_f[:, k, :], hT[:, k, :], k == 0, k == DC - 1)
            mark(last, "ab_f")
            for c in range(4):
                pe.wait_ge(uc_ready, c + 1)
                ps = fill(f"lr{c}")
                for j in range(2):
                    last = mm(ps[:, j * S:(j + 1) * S], lru_w[:, 4 * j + c, :], uc[:, c, :], True, True)
                mark(last, f"lr{c}")

            def fox_ready():
                copied(pe, *(f"ab_{t}{i}" for t in "qkv" for i in range(2)))
                pe.wait_ge(f_ready, 1)

            attention("fox", fox_ready)
            pe.wait_ge(lru_out, 4)
            copied(pe, *outs("fox"))
            columns("abo0_", yT)
            columns("abo1_", yT)

            def cross(layer):
                if layer == 0:
                    norm("mem")
                pe.wait_ge(mn_ready, 8 * (layer + 1))
                columns(f"xk{layer}_0_", mn)
                norm(f"xa{layer}")
                columns(f"xk{layer}_1_", mn)
                for i in range(2):
                    w, u = take()
                    rows(f"xv{layer}_{i}_", mn, w, u, 0, 512)
                ready = chunk_wait(h_ready)
                columns(f"xq{layer}_0_", hT, ready=ready)
                columns(f"xq{layer}_1_", hT)
                attention(f"xa{layer}", lambda: copied(
                    pe, *(f"x{t}{layer}_{i}_{j}" for t in "qkv" for i in range(2) for j in range(2))))
                copied(pe, *outs(f"xa{layer}"))
                columns(f"xo{layer}_0_", yT)
                columns(f"xo{layer}_1_", yT)

            def mlp(layer):
                norm(f"mlp{layer}")
                ready = chunk_wait(h_ready)
                for i in range(8):
                    columns(f"up{layer}_{i}_", hT, ready=ready if i == 0 else None)
                for side_ in range(2):
                    names = [f"dn{layer}_{side_}_{f}" for f in range(4)]
                    banks = [fill(nm, f) for f, nm in enumerate(names)]
                    for g in range(4):
                        w, u = take()
                        for f in range(4):
                            for k in range(DC):
                                if side_ == 0 and f == 0 and k % 2 == 0:
                                    pe.wait_ge(hid_ready, 16 * layer + 4 * g + k // 2 + 1)
                                last = mm(banks[f][:, 0:S], w[:, k, f * P:(f + 1) * P],
                                          hid[:, 8 * g + k, :], g == 0 and k == 0, g == 3 and k == DC - 1)
                            if g == 3 or f == 3:
                                mark(last, names[f], g == 3, u if f == 3 else None)

            cross(0)
            mlp(0)

            norm("cd")
            ready = chunk_wait(h_ready)
            columns("cd_qc", hT, ready=ready)
            columns("cd_kc", hT)
            w, u = take()
            rows("cd_vc", hT, w, u, 0, 512)
            columns("cd_qd", hT)
            w, u = take()
            twice("cd_kd", w)
            rows("cd_vd", hT, w, u, 2 * P, P)
            for r in range(7):
                copied(pe, *(("cd_qc0", "cd_qc1", "cd_kc0", "cd_kc1", "cd_qd0", "cd_qd1")[r:r + 1]
                             or ("cd_kd0", "cd_kd1")))
                ps = fill(f"rot{r}")
                mark(mm(ps, con("rot1"), zr[:, 2 * r:2 * r + 2, :], True, True), f"rot{r}")

            def cd_ready():
                copied(pe, "cd_vc0", "cd_vc1", "cd_vd0", "cd_vd1")
                pe.wait_ge(rot_ready, 7)

            attention("dil", cd_ready)
            attention("swa", lambda: None)
            copied(pe, *outs("dil"), *outs("swa"))
            columns("cdo0_", yT)
            columns("cdo1_", yT)
            cross(1)
            mlp(1)

            pe.wait_ge(c_ready, 1)
            ps = fill("mod")
            for i in range(12):
                w, u = take()
                for f in range(4):
                    for k in range(DC):
                        last = mm(ps[:, 4 * i + f:4 * i + f + 1], w[:, k, f * P:(f + 1) * P],
                                  csil[:, k:k + 1], k == 0, k == DC - 1)
                mark(last, "mod", i == 11, u)

            norm("final")
            norm("n1")
            ready = chunk_wait(h_ready)
            for tag in ("dq", "dk", "dv"):
                columns(tag, hT, ready=ready)
                ready = None
            ps = fill("ba")
            for t in range(TT):
                for k in range(DC):
                    last = mm(ps[:, 32 * t:32 * t + 32], hT[:, k, t * P:(t + 1) * P], w_ba[:, k, :], k == 0, k == DC - 1)
            mark(last, "ba")
            columns("aq", hT)
            w, u = take()
            twice("ak", w)
            rows("av", hT, w, u, 2 * P, P)
            columns("dz", hT)
            for r in range(3):
                pe.wait_ge(l2_sq, r + 1)
                ps = fill(f"qn{r}")
                mark(mm(ps, blk, PAIRS[r][1], True, True), f"qn{r}")
            for r in range(3):
                pe.wait_ge(l2_ready, r + 1)
                ps = fill(f"rotg{r}")
                mark(mm(ps, con("rot2"), PAIRS[r][0], True, True), f"rotg{r}")
            for r in range(4):
                pe.wait_ge(l2_sq, 4 + r)
                ps = fill(f"l2{r}")
                mark(mm(ps, blk, DPAIRS[r][1], True, True), f"l2{r}")

            def gqa_ready():
                pe.wait_ge(rot_ready, 10)
                copied(pe, "av0", "av1")

            attention("gqa", gqa_ready)

            pe.wait_ge(l2_ready, 7)
            pe.wait_ge(cvs_ready, 3)
            for i in range(2):
                for t in range(TT):
                    ps = fill(f"tok{i}{t}")
                    for c in range(4):
                        last = nc.tensor.transpose(ps[:, c * P:(c + 1) * P], cv[:, 4 + 4 * i + c, t * P:(t + 1) * P], ident)
                    mark(last, f"tok{i}{t}")
            pe.wait_ge(g_ready, 1)
            ps = fill("gc")
            for t in range(TT):
                for d in range(2):
                    mm(ps[:, 16 * t + 8 * d:16 * t + 8 * d + 8], cum[:, d, :], gl[:, t, 8 * d:8 * d + 8], True, True)
                last = mm(ps[:, 32 + 16 * t:48 + 16 * t], ones, gl[:, t, :], True, True)
            mark(last, "gc")
            copied(pe, "tok00", "tok01", "tok10", "tok11")

            for h0 in range(0, 8, 2):
                pair = (h0, h0 + 1)
                for h in pair:
                    r, c = half(h), h // 2
                    ps = fill(f"kk{h}")
                    for t in range(TT):
                        tok = slice(t * P, (t + 1) * P)
                        mm(ps[:, t * P:(t + 1) * P], cv[r, 4 + c, tok], cv[r, 4 + c, tok], True, True)
                        last = mm(ps[:, (2 + t) * P:(3 + t) * P], cv[r, 4 + c, tok], cv[r, c, tok], True, True)
                    mark(last, f"kk{h}")
                    ps = fill(f"gr{h}")
                    for d in range(2):
                        for t in range(TT):
                            j = 2 * d + t
                            last = mm(ps[:, j * P:(j + 1) * P],
                                      gl[:, t, 8 * d + h:8 * d + h + 1].broadcast_to([P, P]), cum[:, d, :], True, True)
                    mark(last, f"gr{h}")
                for h in pair:
                    pe.wait_ge(TT_ready, h + 1)
                    ps = fill(f"T0_{h}")
                    for j in range(4):
                        last = nc.tensor.transpose(ps[:, j * P:(j + 1) * P], d_TT[h % 2][:, j, :], ident)
                    mark(last, f"T0_{h}")
                for l in range(1, NLEV):
                    for i, h in enumerate(pair):
                        e = h % 2
                        pe.wait_ge(LM_ready, NLEV * h0 + 2 * l + i + 1)
                        copied(pe, f"TX{h}_{l - 1}" if l > 1 else f"T0_{h}")
                        ps = fill(f"X{h}_{l}", 4 + e)
                        for j in range(4):
                            last = mm(ps[:, j * P:(j + 1) * P], d_LM[e][:, j, :], d_T[e][:, j, :], True, True)
                        mark(last, f"X{h}_{l}")
                    for i, h in enumerate(pair):
                        e = h % 2
                        copied(pe, f"X{h}_{l}")
                        if l > 1:
                            copied(pe, f"XT{h}_{l - 1}")
                        if l < NLEV - 1:
                            ps = fill(f"TX{h}_{l}")
                            for j in range(4):
                                last = mm(ps[:, j * P:(j + 1) * P], d_TT[e][:, j, :], d_X[e][:, j, :], True, True)
                            mark(last, f"TX{h}_{l}")
                        ps = fill(f"XT{h}_{l}")
                        for j in range(4):
                            last = mm(ps[:, j * P:(j + 1) * P], d_X[e][:, j, :], d_TT[e][:, j, :], True, True)
                        mark(last, f"XT{h}_{l}")
                for i, h in enumerate(pair):
                    e = h % 2
                    copied(pe, f"XT{h}_{NLEV - 1}")
                    ps = fill(f"vn{h}")
                    for d in range(2):
                        last = mm(ps[:, d * HD:(d + 1) * HD], d_TT[e][:, 2 * d + d, :], vtok[:, d, h * HD:(h + 1) * HD], True, True)
                    mark(last, f"vn{h}")
                for i, h in enumerate(pair):
                    e = h % 2
                    copied(pe, f"vn{h}")
                    pe.wait_ge(kd_ready, h + 1)
                    ps = fill(f"st{h}")
                    for d in range(2):
                        last = mm(ps[half(h), d * HD:(d + 1) * HD], d_kd[e][:, d, :], d_vn[e][:, 2 * d + d, :], True, True)
                    mark(last, f"st{h}")
                for i, h in enumerate(pair):
                    e, r = h % 2, half(h)
                    copied(pe, f"st{h}")
                    pe.wait_ge(kg_ready, 2 * h + 2)
                    ps = fill(f"ks{h}")
                    for d in range(2):
                        last = mm(ps[:, d * HD:(d + 1) * HD], d_kg[e][r, d, :], d_S[e][r, d, :], True, True)
                    mark(last, f"ks{h}")
                for i, h in enumerate(pair):
                    e = h % 2
                    copied(pe, f"ks{h}")
                    ps = fill(f"vm{h}")
                    for d in range(2):
                        last = mm(ps[:, d * HD:(d + 1) * HD], d_TT[e][:, 2 * d + second(d), :], d_v2[e][:, d, :], True, True)
                    mark(last, f"vm{h}")
                for i, h in enumerate(pair):
                    e, r = h % 2, half(h)
                    copied(pe, f"vm{h}")
                    ps = fill(f"do{h}", 6 + e)
                    for t in range(TT):
                        o, d2 = ps[r, t * P:(t + 1) * P], 1 - t
                        mm(o, d_vn[e][:, t, :], d_AT[e][:, t, :], True, False)
                        mm(o, d_vn[e][:, 2 + t, :], d_AT[e][:, 2 + t, :], False, False)
                        last = mm(o, d_S[e][r, d2, :], d_qg[e][r, d2, :], False, True)
                    mark(last, f"do{h}")

            for r in range(2):
                pe.wait_ge(l2_sq, 8 + r)
                ps = fill(f"on{r}")
                mark(mm(ps, blk, tA[:, 2 * r:2 * r + 2, :], True, True), f"on{r}")
            for i in range(4):
                columns(f"sg{i}_", hT)
            copied(pe, *outs("gqa"))
            w, u = take()
            for b in range(4):
                ps = fill(f"au{b}")
                for j in range(2):
                    for k in range(4):
                        last = mm(ps[:, j * S:(j + 1) * S], w[:, k, (2 * b + j) * P:(2 * b + j + 1) * P], gaT[:, k, :], k == 0, k == 3)
                mark(last, f"au{b}", u=u if b == 3 else None)
            pe.wait_ge(dn_ready, 2)
            w, u = take()
            for b in range(4):
                ps = fill(f"du{b}")
                for j in range(2):
                    for k in range(4):
                        last = mm(ps[:, j * S:(j + 1) * S], w[:, k, (2 * b + j) * P:(2 * b + j + 1) * P], dnT[:, k, :], k == 0, k == 3)
                mark(last, f"du{b}", u=u if b == 3 else None)
            columns("wo0_", sga, ready=lambda k: pe.wait_ge(mg_ready, k // 2 + 1))
            columns("wo1_", sga)

            norm("n2", sgd)
            ready = chunk_wait(h_ready)
            ps = fill("router")
            for t in range(TT):
                for k in range(DC):
                    if t == 0:
                        ready(k)
                    last = mm(ps[:, 16 * t:16 * t + 16], hT[:, k, t * P:(t + 1) * P], w_rt[:, k, :], k == 0, k == DC - 1)
            mark(last, "router")
            for t in range(TT):
                for i in range(2):
                    ps = fill(f"h2_{t}{i}")
                    for c in range(4):
                        last = nc.tensor.transpose(ps[:, c * P:(c + 1) * P], hT[:, 4 * i + c, t * P:(t + 1) * P], ident)
                    mark(last, f"h2_{t}{i}")
            pe.wait_ge(aff_ready, 1)
            ps = fill("affT")
            for t in range(TT):
                last = nc.tensor.transpose(ps[0:NE, t * P:(t + 1) * P], aff[:, t, :], ident)
            mark(last, "affT")
            pe.wait_ge(sel_ready, 1)
            ps = fill("selT")
            for t in range(TT):
                last = nc.tensor.transpose(ps[:, 16 * t:16 * t + 16], rw[2][:, t * P:(t + 1) * P], ident[0:NE, 0:NE])
            mark(last, "selT")
            pe.wait_ge(P_ready, 1)
            copied(pe, "h2_00", "h2_01", "h2_10", "h2_11")
            for c in range(DC):
                ps = fill(f"xe{c}")
                for t in range(TT):
                    last = mm(ps, h2t[:, t, c * P:(c + 1) * P], Ph[:, t, :], t == 0, t == 1)
                mark(last, f"xe{c}")
            pe.wait_ge(PG_ready, 1)
            for g in range(4):
                ps = fill(f"pg{g}")
                for t in range(TT):
                    last = nc.tensor.transpose(ps[:, t * P:(t + 1) * P], Pg[:, t, g * P:(g + 1) * P], ident)
                mark(last, f"pg{g}")

            for b in (4, 5, 6):
                pe.wait_ge(freed[b], taken[b])
            with pe.Fori(0, NE) as e:
                pe.wait_ge(xs_ready, e + 1)
                for j in range(6):
                    if j == 4:
                        pe.wait_ge(hg_ready, e + 2)
                        pe.wait_ge(ye_ready, e + 1)
                    pe.wait_ge(loaded[ESLOT[j]], e * 16 + 16 * (EBASE[j] + 1))
                    at_s = ESLOT[j] * UNIT
                    w = ring[:, at_s:at_s + UNIT].rearrange("p (c n) -> p c n", n=512)
                    src = xs if j < 4 else hg
                    for f in range(4):
                        c = (4 * (j % 2) + f) * CAP
                        for k in range(DC):
                            last = mm(pb[:, 4 + j // 2, c:c + CAP], w[:, k, f * P:(f + 1) * P], src[:, k, :],
                                      k == 0, k == DC - 1)
                    last.then_inc(filled[4 + j // 2], 1)

            pe.wait_ge(ye_ready, NE + 1)
            for g in range(4):
                for i in range(2):
                    ps = fill(f"yt{g}{i}")
                    for c in range(4):
                        last = nc.tensor.transpose(ps[:, c * P:(c + 1) * P], ye[:, 4 * i + c, g * P:(g + 1) * P], ident)
                    mark(last, f"yt{g}{i}")
            copied(pe, *(f"yt{g}{i}" for g in range(4) for i in range(2)), *(f"pg{g}" for g in range(4)))
            for c in range(4):
                ps = fill(f"fin{c}")
                for j in range(2):
                    for g in range(4):
                        last = mm(ps[:, j * S:(j + 1) * S], ytok[:, g, (2 * c + j) * P:(2 * c + j + 1) * P], PGt[:, g, :],
                                  g == 0, g == 3)
                mark(last, f"fin{c}")

        EMARK = {b: marks[b] for b in (4, 5, 6)}

        def full(eng, name):
            b, m, _ = fillings[name]
            eng.wait_ge(filled[b], m)
            return pb[:, b, :], freed[b]

        def pairs(ps):
            return ps.rearrange("p (a b) -> p a b", a=2)

        def fours(ps):
            return ps.rearrange("p (a b) -> p a b", a=4)

        @block.sync
        def _(sp):
            sp.dma_start(xT, a["xT"].rearrange("(c p) t -> p c t", p=P)).then_inc(x_in, 16)
            for u in range(NDENSE):
                w, r0, nr, c0, ncol = units[u]
                if u >= SLOTS:
                    b, m = unit_read[u - SLOTS]
                    sp.wait_ge(filled[b], m)
                sp.dma_start(slot_ap(u), w[r0:r0 + nr, c0:c0 + ncol].rearrange("(c p) n -> p c n", p=P)
                             ).then_inc(loaded[u % SLOTS], 16)

            def expert_unit(e, j):
                w = a[("w_gate_2", "w_up_2", "w_down_2")[j // 2]]
                at_s = ESLOT[j] * UNIT
                sp.dma_start(ring[:, at_s:at_s + UNIT].rearrange("p (c n) -> p c n", n=512),
                             w[bass.ds(e, 1), :, (j % 2) * 512:(j % 2 + 1) * 512].rearrange("a (c p) n -> p (a c) n", p=P)
                             ).then_inc(loaded[ESLOT[j]], 16)

            for j in range(6):
                b, m = unit_read[NDENSE + j - SLOTS]
                sp.wait_ge(filled[b], m)
                expert_unit(0, j)
            with sp.Fori(1, NE) as e:
                for j in range(6):
                    b = 4 + j // 2
                    sp.wait_ge(filled[b], (e - 1) * 2 + (EMARK[b] + j % 2 + 1))
                    expert_unit(e, j)
            for c in range(4):
                copied(sp, f"fin{c}")
                sp.dma_start(out.rearrange("(c p) t -> p c t", p=P)[:, 2 * c:2 * c + 2, :],
                             xT[:, 2 * c:2 * c + 2, :]).then_inc(out_sent, 16)
            sp.wait_ge(out_sent, 64)

        @block.gpsimd
        def _(pool):
            pool.wait_ge(lru_out, 4)
            pool.dma_start(memT, a["memT"].rearrange("(c p) t -> p c t", p=P)).then_inc(mem_in, 16)
            for h0 in range(0, 8, 2):
                for l in range(NLEV):
                    for h in (h0, h0 + 1):
                        e, r = h % 2, half(h)
                        if l == 0:
                            copied(pool, f"kk{h}")
                            if h0:
                                full(pool, f"X{h - 2}_{NLEV - 1}")
                        elif l == 1:
                            pool.wait_ge(TT_ready, h + 1)
                        else:
                            full(pool, f"X{h}_{l - 1}")
                        for d in range(2):
                            ins = nc.gpsimd.tensor_tensor(
                                d_LM[e][:, 2 * d:2 * d + 2, :], d_LT[e][:, 2 * d:2 * d + 2, :],
                                lev[:, l, d, :].unsqueeze(1).broadcast_to([P, 2, P]), ALU.mult)
                        ins.then_inc(LM_ready, 1)
                    if l:
                        continue
                    for h in (h0, h0 + 1):
                        e, r = h % 2, half(h)
                        copied(pool, f"gr{h}")
                        pool.wait_ge(*((LM_ready, NLEV * h0 + 2) if h == h0 else (kg_ready, 2 * h)))
                        for d in range(2):
                            tok = slice(second(d) * P, (second(d) + 1) * P)
                            ins = nc.gpsimd.tensor_tensor(d_kg[e][r, d, :], cv[r, 4 + h // 2, tok], d_qg[e][r, d, :], ALU.mult)
                        ins.then_inc(kg_ready, 1)
                        pool.wait_ge(kg_ready, 2 * h + 1)
                        for d in range(2):
                            tok = slice(second(d) * P, (second(d) + 1) * P)
                            ins = nc.gpsimd.tensor_tensor(d_qg[e][r, d, :], cv[r, h // 2, tok], d_qg[e][r, d, :], ALU.mult)
                        ins.then_inc(kg_ready, 1)
                    pool.wait_ge(kg_ready, 2 * h0 + 4)
            copied(pool, *(f"xe{c}" for c in range(DC)))
            with pool.Fori(0, NE) as e:
                pool.wait_ge(hg_ready, e + 1)
                nc.gpsimd.tensor_copy(xs, xe[:, :, bass.ds(e * CAP, CAP)]).then_inc(xs_ready, 1)

        @block.scalar
        def _(act):
            def fn(o, i, f, **kw):
                return nc.scalar.activation(o, i, f, **kw)

            steps = [0]

            def link(ins):
                steps[0] += 1
                ins.then_inc(act_step, 1)
                act.wait_ge(act_step, steps[0])

            def copy(name, dst, src=lambda ps: ps, scale=1.0):
                ps, free = full(act, name)
                fn(dst, src(ps), ACT.Copy, scale=scale).then_inc(free, 1)

            def squares(src, names=None, signal=None, base=0, dst=sq):
                for c in range(DC):
                    if names is not None:
                        copied(act, names[c])
                    if signal is not None:
                        act.wait_ge(signal, base + c + 1)
                    fn(dst[:, c, :], src[:, c, :], ACT.Square).then_inc(norm_sq, 1)

            def root(tag):
                ps, free = full(act, f"norm_{tag}")
                fn(rt[:, :], ps[:, 0:S], ACT.Sqrt, scale=1.0 / D, bias=eps).then_inc(free, 1)

            def residual(tag):
                return [f"{tag}{c // 4}_{c % 4 // 2}" for c in range(DC)]

            pcount = [0]

            def attention(stage, out_of):
                h0, heads, causal, wide = FIRST_HEAD[stage], HEADS[stage], stage in CAUSAL, stage in WIDE

                def exps(h):
                    n = h0 + h
                    e = n % 2
                    act.wait_ge(mx_ready, n + 1)
                    ps, free = full(act, f"s{n}")
                    for qb in range(2):
                        nk = P if causal and qb == 0 else S
                        src = sm[:, e, qb, 0:nk] if causal else pairs(ps)[:, qb, :]
                        ins = fn(pr[:, e, qb, 0:nk], src, ACT.Exp, bias=nmx[:, e, qb:qb + 1],
                                 accum_out=den[:, e, qb:qb + 1])
                        if not causal and qb:
                            ins.then_inc(free, 1)
                    if stage == "swa":
                        ins = fn(es[:, e, :], nmx[:, e, :], ACT.Exp, bias=col("sink", h))
                    if causal:
                        ins.then_inc(p_ready, 1)

                def turned(h):
                    n = h0 + h
                    ps, _ = full(act, f"t{n}")
                    w = 384 if causal else 512
                    b = fillings[f"t{n}"][0]
                    fn(pT[:, n % 2, 0:w], ps[:, 0:w], ACT.Copy).then_inc(freed[b], 1)

                exps(0)
                for h in range(heads):
                    if h + 1 < heads:
                        exps(h + 1)
                    turned(h)
                    if wide:
                        copy(f"o{h0 + h}", yT[:, 2 * h:2 * h + 2, :], pairs)
                    elif h % 2:
                        copy(f"o{h0 + h - 1}", out_of(h // 2), lambda ps: ps[:, 0:S])

            for dst, name in ((cols, "cols"), (cons, "cons"), (small_w, "small_w"), (lru_w_, "lru_w")):
                act.dma_start(dst[:, :], a[name]).then_inc(small_in, 16)
            act.wait_ge(small_in, 64)
            act.wait_ge(sp_abs, 1)
            fn(sp_t[1], sp_t[0], ACT.Exp, scale=-1.0).then_inc(sp_exp, 1)
            fn(csil, col("c", 0, 8), ACT.Tanh, scale=0.5).then_inc(c_tanh, 1)

            act.wait_ge(x_in, 16)
            squares(xT)
            root("ab")
            act.wait_ge(pads, 1)
            for i in range(2):
                copy(f"ab_u{i}", up[:, 2 * i:2 * i + 2, 3:3 + S], pairs)
            for i in range(2):
                copy(f"ab_gate{i}", gt[:, 2 * i:2 * i + 2, :], pairs)
            for i in range(2):
                copy(f"ab_q{i}", qT[:, 2 * i:2 * i + 2, :], pairs, 0.125)
            for i in range(2):
                copy(f"ab_k{i}", kT[:, 2 * i:2 * i + 2, :], pairs)
            for t in range(TT):
                copy(f"ab_v{t}", vt[:, t, 0:512])
            act.wait_ge(sp_abs, 2)
            fn(fz[1], fz[0], ACT.Exp, scale=-1.0).then_inc(sp_exp, 1)
            act.wait_ge(hb_ready, 1)
            for c in range(4):
                ps, free = full(act, f"lr{c}")
                fn(l_r[:, c, :], ps[:, 0:S], ACT.Tanh, scale=0.5, bias=hba[:, c:c + 1])
                fn(l_i[:, c, :], ps[:, S:2 * S], ACT.Tanh, scale=0.5, bias=hbi[:, c:c + 1]).then_inc(free, 1)
            act.wait_ge(gin_ready, 1)
            fn(l_g, l_g, ACT.Tanh, scale=math.sqrt(2.0 / math.pi)).then_inc(gth_ready, 1)
            act.wait_ge(ly_ready, 4)
            fn(l_a, l_r, ACT.Exp, scale=-1.0)
            fn(l_r, l_r, ACT.Tanh).then_inc(la_ready, 1)
            act.wait_ge(lw_ready, 1)
            fn(l_r, l_r, ACT.Sqrt, scale=0.5).then_inc(lx_ready, 1)
            attention("fox", lambda c: yT[:, 4 + c, :])

            def cross(layer, names):
                if layer == 0:
                    act.wait_ge(mem_in, 16)
                    squares(memT)
                    root("mem")
                squares(xT, names)
                for j in range(2):
                    copy(f"xk{layer}_0_{j}", kT[:, 2 * j:2 * j + 2, :], pairs)
                root(f"xa{layer}")
                for j in range(2):
                    copy(f"xk{layer}_1_{j}", kT[:, 4 + 2 * j:6 + 2 * j, :], pairs)
                for i in range(2):
                    for t in range(TT):
                        copy(f"xv{layer}_{i}_{t}", vt[:, t, 512 * i:512 * (i + 1)])
                for i in range(4):
                    copy(f"xq{layer}_{i // 2}_{i % 2}", qT[:, 2 * i:2 * i + 2, :], pairs, 1.0 / 16)
                attention(f"xa{layer}", None)

            def mlp(layer):
                squares(xT, residual(f"xo{layer}_"))
                root(f"mlp{layer}")
                for n in range(16):
                    copied(act, f"up{layer}_{n // 2}_{n % 2}")
                    fn(hid[:, 2 * n:2 * n + 2, :], pairs(hrelu[:, n % 2, :]), ACT.Square).then_inc(hid_ready, 1)

            cross(0, residual("abo"))
            mlp(0)
            squares(xT, [f"dn0_{c // 4}_{c % 4}" for c in range(DC)])
            root("cd")
            for i in range(2):
                copy(f"cd_qc{i}", zr[:, 2 * i:2 * i + 2, :], pairs, 0.125)
            for i in range(2):
                copy(f"cd_kc{i}", zr[:, 4 + 2 * i:6 + 2 * i, :], pairs)
            for t in range(TT):
                copy(f"cd_vc{t}", vt[:, t, 0:512])
            for i in range(2):
                copy(f"cd_qd{i}", zr[:, 8 + 2 * i:10 + 2 * i, :], pairs, 0.125)
            for g in range(2):
                copy(f"cd_kd{g}", zr[:, 12 + g, :], lambda ps: ps[:, 0:S])
            for t in range(TT):
                copy(f"cd_vd{t}", vt[:, t, 512:640], lambda ps: ps[:, 0:P])
            attention("dil", lambda c: yT[:, c, :])
            attention("swa", lambda c: yT[:, 4 + c, :])
            cross(1, residual("cdo"))
            mlp(1)

            squares(xT, [f"dn1_{c // 4}_{c % 4}" for c in range(DC)])
            root("final")
            squares(xT, signal=fin_ready)
            root("n1")
            act.wait_ge(pads, 2)
            for i, tag in enumerate(("dq0", "dq1", "dk0", "dk1", "dv0", "dv1")):
                copy(tag, cp[:, 2 * i:2 * i + 2, 2:2 + S], pairs)
            ps, _ = full(act, "ba")
            fn(beta, ps[:, 0:64].rearrange("p (t n) -> p t n", t=2)[:, :, 0:NE], ACT.Tanh, scale=0.5).then_inc(ba_th, 1)
            for i in range(2):
                copy(f"aq{i}", gq[:, 2 * i:2 * i + 2, :], pairs)
            for g in range(2):
                copy(f"ak{g}", gk[:, g, :], lambda ps: ps[:, 0:S])
            for t in range(TT):
                copy(f"av{t}", gv[:, t, :], lambda ps: ps[:, 0:P])
            for r in range(3):
                copied(act, *(("aq0",), ("aq1",), ("ak0", "ak1"))[r])
                fn(PAIRS[r][1], PAIRS[r][0], ACT.Square).then_inc(l2_sq, 1)
            act.wait_ge(sp_abs, 3)
            fn(sp_a[1], sp_a[0], ACT.Exp, scale=-1.0).then_inc(sp_exp, 1)
            fn(alog, col("a_log", 0, NE), ACT.Exp).then_inc(sp_exp, 1)
            for i in range(2):
                ps, _ = full(act, f"dz{i}")
                fn(dzt[:, 2 * i:2 * i + 2, :], pairs(ps), ACT.Tanh, scale=0.5).then_inc(dzt_ready, 1)
            for g in range(3):
                act.wait_ge(cv_ready, 4 * (g + 1))
                if g:
                    act.wait_ge(cvs_ready, g)
                fn(cth, cv[:, 4 * g:4 * g + 4, :], ACT.Tanh, scale=0.5).then_inc(cvt_ready, 1)
            roots = [0]

            def head_root(name, scale):
                if roots[0] >= 2:
                    act.wait_ge(l2_ready, roots[0] - 1)
                ps, free = full(act, name)
                fn(rt2[:, roots[0] % 2, :, :], pairs(ps), ACT.Sqrt, scale=scale, bias=eps).then_inc(free, 1)
                roots[0] += 1

            for r in range(3):
                head_root(f"qn{r}", 1.0 / HD)
            for r in range(4):
                act.wait_ge(cvs_ready, 3)
                fn(DPAIRS[r][1], DPAIRS[r][0], ACT.Square).then_inc(l2_sq, 1)
            for r in range(4):
                head_root(f"l2{r}", 0.25)
            attention("gqa", lambda c: gaT[:, c, :])
            for t in range(TT):
                copy(f"tok0{t}", ktok[:, t, :])
            for t in range(TT):
                copy(f"tok1{t}", vtok[:, t, :], scale=0.5)
            act.wait_ge(ekd_ready, 1)
            fn(ekd, ekd, ACT.Exp).then_inc(ekx_ready, 1)
            for h0 in range(0, 8, 2):
                pair = (h0, h0 + 1)
                for h in pair:
                    e, r = h % 2, half(h)
                    ps, free = full(act, f"gr{h}")
                    act.wait_ge(dd_ready, h + 1)
                    fn(d_LT[e], d_LT[e], ACT.Exp).then_inc(dec_ready, 1)
                    for d in range(2):
                        ins = fn(d_qg[e][r, d, :], fours(ps)[r, 2 * d + second(d), :], ACT.Exp)
                    ins.then_inc(free, 1)
                for h in pair:
                    copy(f"T0_{h}", d_T[h % 2], fours)
                for l in range(1, NLEV):
                    for h in pair:
                        copy(f"X{h}_{l}", d_X[h % 2], fours)
                for h in pair:
                    r = half(h)
                    copy(f"st{h}", d_S[h % 2][r, :, :], lambda ps: ps[r, 0:P].rearrange("p (d n) -> p d n", d=2))
                for h in pair:
                    r = half(h)
                    copy(f"do{h}", d_o[r, h // 2, :], lambda ps: ps[r, 0:S])
            for r in range(2):
                copied(act, f"do{4 * r + 2}", f"do{4 * r + 3}")
                fn(tA[:, 2 * r:2 * r + 2, :], d_o[:, 2 * r:2 * r + 2, :], ACT.Square).then_inc(l2_sq, 1)
            for r in range(2):
                head_root(f"on{r}", 1.0 / HD)
            for n in range(8):
                ps, free = full(act, f"sg{n // 2}_{n % 2}")
                dst = (sga, sgd)[n // 4]
                fn(dst[:, 2 * (n % 4):2 * (n % 4) + 2, :], pairs(ps), ACT.Tanh, scale=0.5).then_inc(free, 1)

            squares(xT, residual("wo"), dst=sgd)
            root("n2")
            act.wait_ge(rt_mx, 1)
            ps, free = full(act, "router")
            for t in range(TT):
                ins = fn(aff[:, t, :], ps[:, NE * t:NE * t + NE], ACT.Exp, bias=nmx[:, 0, t:t + 1],
                         accum_out=raff[:, t:t + 1])
            ins.then_inc(free, 1)
            for t in range(TT):
                for i in range(2):
                    copy(f"h2_{t}{i}", h2t[:, t, 512 * i:512 * (i + 1)])
            for c in range(0, DC, 2):
                copy(f"xe{c}", xe[:, c, :])
            for g in range(4):
                copy(f"pg{g}", PGt[:, g, :], lambda ps: ps[:, 0:S])
            nc.scalar.nop().then_inc(ye_ready, 1)
            with act.Fori(0, NE) as e:
                act.wait_ge(filled[4], e * 2 + (EMARK[4] + 2))
                fn(tg, pb[:, 4, 0:S].rearrange("p (c n) -> p c n", n=CAP), ACT.Tanh, scale=0.5).then_inc(eth_ready, 1)
                act.wait_ge(filled[6], e * 2 + (EMARK[6] + 2))
                fn(ye[:, :, bass.ds(e * CAP, CAP)], pb[:, 6, 0:S].rearrange("p (c n) -> p c n", n=CAP),
                   ACT.Copy).then_inc(ye_ready, 1)
            for g in range(4):
                copy(f"yt{g}0", ytok[:, g, 0:512])

        @block.vector
        def _(dve):
            V = nc.vector
            steps = [0]

            def link(ins):
                steps[0] += 1
                ins.then_inc(dve_step, 1)
                dve.wait_ge(dve_step, steps[0])

            def invert(tag):
                copied(dve, f"norm_{tag}")
                link(V.reciprocal(rs[:, :], rt[:, :]))

            def norm(tag, gain, dst=None, signal=None):
                invert(tag)
                for c in range(DC):
                    V.scalar_tensor_tensor((hT if dst is None else dst)[:, c, :], xT[:, c, :], gain(c), rs[:, :],
                                           ALU.mult, ALU.mult).then_inc(h_ready if signal is None else signal, 1)

            def shifted_norm(tag, gain, shift):
                invert(tag)
                for c in range(DC):
                    link(V.scalar_tensor_tensor(hT[:, c, :], xT[:, c, :], gain[:, c:c + 1], rs[:, :], ALU.mult, ALU.mult))
                    V.tensor_scalar(hT[:, c, :], hT[:, c, :], modc[:, shift + c:shift + c + 1], None, ALU.add).then_inc(h_ready, 1)

            def add(tag):
                for i in range(4):
                    ps, free = full(dve, f"{tag}{i // 2}_{i % 2}")
                    V.tensor_tensor(xT[:, 2 * i:2 * i + 2, :], xT[:, 2 * i:2 * i + 2, :], pairs(ps), ALU.add).then_inc(free, 1)

            def log1p(t, e_count, res, z):
                dve.wait_ge(sp_exp, e_count)
                link(V.tensor_scalar(t[0], t[1], 2.0, None, ALU.add))
                link(V.reciprocal(t[0], t[0]))
                link(V.tensor_tensor(t[0], t[0], t[1], ALU.mult))
                link(V.tensor_tensor(t[1], t[0], t[0], ALU.mult))
                link(V.tensor_scalar(t[2], t[1], 1.0 / 17, None, ALU.mult))
                for k in (15, 13, 11, 9, 7, 5, 3):
                    link(V.scalar_tensor_tensor(t[2], t[2], 1.0 / k, t[1], ALU.add, ALU.mult))
                link(V.scalar_tensor_tensor(t[2], t[2], 1.0, t[0], ALU.add, ALU.mult))
                link(V.tensor_scalar(t[0], z, 0.0, None, ALU.max))
                link(V.scalar_tensor_tensor(res, t[2], 2.0, t[0], ALU.mult, ALU.add))

            def attention(stage):
                h0, heads, mask = FIRST_HEAD[stage], HEADS[stage], CAUSAL.get(stage)

                def row_max(h):
                    n = h0 + h
                    e = n % 2
                    ps, free = full(dve, f"s{n}")
                    if mask is None:
                        V.tensor_reduce(nmx[:, e, :], pairs(ps), AX.X, ALU.max, negate=True).then_inc(mx_ready, 1)
                        return
                    for qb in range(2):
                        nk = P if qb == 0 else S
                        start = col("sink", h) if stage == "swa" else NEG
                        ins = V.tensor_tensor_reduce(
                            out=sm[:, e, qb, 0:nk], in0=ps[:, qb * S:qb * S + nk], in1=con(mask, 2, S)[:, qb, 0:nk],
                            scale=1.0, scalar=start, op0=ALU.add, op1=ALU.max, accum_out=mxr[:, e, qb:qb + 1])
                    ins.then_inc(free, 1)
                    copied(dve, f"s{n}")
                    V.tensor_scalar(nmx[:, e, :], mxr[:, e, :], -1.0, None, ALU.mult).then_inc(mx_ready, 1)

                def scale(h):
                    n = h0 + h
                    e = n % 2
                    if mask is None:
                        copied(dve, f"s{n}")
                    else:
                        masked[0] += 1
                        dve.wait_ge(p_ready, masked[0])
                    if stage == "swa":
                        link(V.tensor_tensor(den[:, e, :], den[:, e, :], es[:, e, :], ALU.add))
                    link(V.reciprocal(den[:, e, :], den[:, e, :]))
                    for qb in range(2):
                        nk = P if mask and qb == 0 else S
                        ins = V.tensor_scalar(pr[:, e, qb, 0:nk], pr[:, e, qb, 0:nk], den[:, e, qb:qb + 1], None, ALU.mult)
                    ins.then_inc(pn_ready, 1)

                row_max(0)
                for h in range(heads):
                    if h + 1 < heads:
                        row_max(h + 1)
                    scale(h)

            masked = [0]

            dve.wait_ge(small_in, 64)
            link(V.tensor_scalar(sp_t[3], col("lam", 0, 4), -1.0, None, ALU.mult))
            V.scalar_tensor_tensor(sp_t[0], sp_t[3], -1.0, sp_t[3], ALU.mult, ALU.max).then_inc(sp_abs, 1)
            V.memset(up[:, :, 0:3], 0.0).then_inc(pads, 1)
            V.tensor_scalar(hba, col("b_a", 0, 4), 0.5, None, ALU.mult)
            V.tensor_scalar(hbi, col("b_i", 0, 4), 0.5, None, ALU.mult).then_inc(hb_ready, 1)
            V.tensor_scalar(wq8, col("q_norm"), 0.125, None, ALU.mult)
            dve.wait_ge(c_tanh, 1)
            link(V.scalar_tensor_tensor(csil, csil, 1.0, col("c", 0, 8), ALU.add, ALU.mult))
            V.tensor_scalar(csil, csil, 0.5, None, ALU.mult).then_inc(c_ready, 1)
            log1p(sp_t, 1, c4, sp_t[3])
            link(V.tensor_scalar(c4, c4, 4.0, None, ALU.mult))

            norm("ab", lambda c: col("ab_norm", c))
            for c in range(4):
                copied(dve, f"ab_u{c // 2}")
                link(V.tensor_scalar(uc[:, c, :], up[:, c, 0:S], col("conv_w", c), col("conv_b", c), ALU.mult, ALU.add))
                for j in range(1, 4):
                    ins = V.scalar_tensor_tensor(uc[:, c, :], up[:, c, j:j + S], col("conv_w", 4 * j + c), uc[:, c, :],
                                                 ALU.mult, ALU.add)
                    if j < 3:
                        link(ins)
                ins.then_inc(uc_ready, 1)
            ps, free = full(dve, "ab_f")
            V.tensor_scalar(fz[3], ps[0:8, 0:S], col("fox_b")[0:8, :], -1.0, ALU.add, ALU.mult).then_inc(free, 1)
            copied(dve, "ab_f")
            V.scalar_tensor_tensor(fz[0], fz[3], -1.0, fz[3], ALU.mult, ALU.max).then_inc(sp_abs, 1)
            for i in range(4):
                full(dve, f"lr{i}")
            copied(dve, "ab_gate0", "ab_gate1")
            link(V.tensor_tensor(l_g, gt, gt, ALU.mult))
            link(V.tensor_scalar(l_g, l_g, 0.044715, 1.0, ALU.mult, ALU.add))
            V.tensor_tensor(l_g, l_g, gt, ALU.mult).then_inc(gin_ready, 1)
            log1p(fz, 2, fy[0], fz[3])
            V.tensor_tensor_scan(cc, fy[0], fy[0], 0.0, ALU.add, ALU.max).then_inc(f_ready, 1)
            for c in range(4):
                copied(dve, f"lr{c}")
                V.tensor_scalar(l_r[:, c, :], l_r[:, c, :], 1.0, c4[:, c:c + 1], ALU.add, ALU.mult).then_inc(ly_ready, 1)
            link(V.scalar_tensor_tensor(uc, l_i, 1.0, uc, ALU.add, ALU.mult))
            dve.wait_ge(la_ready, 1)
            link(V.tensor_scalar(l_i, l_r, 1.0, None, ALU.add))
            link(V.reciprocal(l_i, l_i))
            V.tensor_tensor(l_r, l_r, l_i, ALU.mult).then_inc(lw_ready, 1)
            dve.wait_ge(gth_ready, 1)
            link(V.scalar_tensor_tensor(gt, l_g, 1.0, gt, ALU.add, ALU.mult))
            dve.wait_ge(lx_ready, 1)
            link(V.tensor_tensor(uc, uc, l_r, ALU.mult))
            for c in range(4):
                ins = V.tensor_tensor_scan(l_i[:, c, :], l_a[:, c, :], uc[:, c, :], 0.0, ALU.mult, ALU.add)
                link(ins)
                V.scalar_tensor_tensor(yT[:, c, :], l_i[:, c, :], 0.5, gt[:, c, :], ALU.mult, ALU.mult).then_inc(lru_out, 1)
            attention("fox")
            add("abo")

            def cross(layer):
                if layer == 0:
                    invert("mem")
                    link(V.tensor_tensor(memT, memT, rs[:, :].unsqueeze(1).broadcast_to([P, DC, S]), ALU.mult))
                for c in range(DC):
                    V.tensor_scalar(mn[:, c, :], memT[:, c, :], col(f"mem_norm{layer}", c), None, ALU.mult).then_inc(mn_ready, 1)
                norm(f"xa{layer}", lambda c: col(f"xa_norm{layer}", c))
                attention(f"xa{layer}")
                add(f"xo{layer}_")

            def mlp(layer):
                norm(f"mlp{layer}", lambda c: col(f"mlp_norm{layer}", c))
                for n in range(16):
                    if n >= 2:
                        dve.wait_ge(hid_ready, 16 * layer + n - 1)
                    ps, free = full(dve, f"up{layer}_{n // 2}_{n % 2}")
                    V.tensor_scalar(hrelu[:, n % 2, :], ps, 0.0, None, ALU.max).then_inc(free, 1)
                for c in range(DC):
                    ps, free = full(dve, f"dn{layer}_{c // 4}_{c % 4}")
                    V.tensor_tensor(xT[:, c, :], xT[:, c, :], ps[:, 0:S], ALU.add).then_inc(free, 1)

            def rotate(name, z, dst, cs, sn, ta, tb):
                ps, free = full(dve, name)
                both = lambda t: con(t).unsqueeze(1).broadcast_to([P, 2, S])
                V.tensor_tensor(ta, z, both(cs), ALU.mult)
                V.tensor_tensor(tb, pairs(ps), both(sn), ALU.mult).then_inc(free, 1)
                copied(dve, name)
                V.tensor_tensor(dst, ta, tb, ALU.add).then_inc(rot_ready, 1)

            cross(0)
            mlp(0)
            norm("cd", lambda c: col("cd_norm", c))
            dsts = [qT[:, 0:2, :], qT[:, 2:4, :], kT[:, 0:2, :], kT[:, 2:4, :], qT[:, 4:6, :], qT[:, 6:8, :], kT[:, 4:6, :]]
            for r in range(7):
                if r:
                    dve.wait_ge(rot_ready, r)
                rotate(f"rot{r}", zr[:, 2 * r:2 * r + 2, :], dsts[r], "cos1", "sin1", ra, rb)
            attention("dil")
            attention("swa")
            add("cdo")
            cross(1)
            mlp(1)

            ps, free = full(dve, "mod")
            V.tensor_tensor(modc, ps[:, 0:48], col("b_ada", 0, 48), ALU.add).then_inc(free, 1)
            copied(dve, "mod")
            V.scalar_tensor_tensor(g1s, modc[:, 8:16], 1.0, col("norm1", 0, 8), ALU.add, ALU.mult)
            V.scalar_tensor_tensor(g2s, modc[:, 32:40], 1.0, col("norm2", 0, 8), ALU.add, ALU.mult)
            link(V.tensor_scalar(hgt1, modc[:, 16:24], 0.5, None, ALU.mult))
            norm("final", lambda c: col("final_norm", c), xT, fin_ready)
            dve.wait_ge(fin_ready, 8)
            shifted_norm("n1", g1s, 0)
            V.memset(cp[:, :, 0:2], 0.0)
            V.memset(cp[:, :, 2 + S:4 + S], 0.0).then_inc(pads, 1)
            for c in range(12):
                copied(dve, ("dq0", "dq1", "dk0", "dk1", "dv0", "dv1")[c // 2])
                link(V.tensor_scalar(cv[:, c, :], cp[:, c, 0:S], col("conv2_w", c), None, ALU.mult))
                for j in range(1, 5):
                    ins = V.scalar_tensor_tensor(cv[:, c, :], cp[:, c, j:j + S], col("conv2_w", 12 * j + c), cv[:, c, :],
                                                 ALU.mult, ALU.add)
                    if j < 4:
                        link(ins)
                ins.then_inc(cv_ready, 1)
                if c == 3:
                    ps, free = full(dve, "ba")
                    dve.wait_ge(ba_th, 1)
                    for t in range(TT):
                        ins = V.tensor_tensor(sp_a[3][:, t, :], ps[:, 32 * t + 16:32 * t + 32], col("dt_bias", 0, NE), ALU.add)
                    ins.then_inc(free, 1)
                    copied(dve, "ba")
                    V.scalar_tensor_tensor(sp_a[0], sp_a[3], -1.0, sp_a[3], ALU.mult, ALU.max).then_inc(sp_abs, 1)
                    link(V.tensor_scalar(beta, beta, 1.0, 0.5, ALU.add, ALU.mult))
            for g in range(3):
                dve.wait_ge(cvt_ready, g + 1)
                V.scalar_tensor_tensor(cv[:, 4 * g:4 * g + 4, :], cth, 1.0, cv[:, 4 * g:4 * g + 4, :],
                                       ALU.add, ALU.mult).then_inc(cvs_ready, 1)
            log1p(sp_a, 4, sp_a[1], sp_a[3])
            for t in range(TT):
                ins = V.scalar_tensor_tensor(gl[:, t, :], sp_a[1][:, t, :], -1.0, alog, ALU.mult, ALU.mult)
            ins.then_inc(g_ready, 1)
            for i in range(2):
                ps, free = full(dve, f"dz{i}")
                dve.wait_ge(dzt_ready, i + 1)
                V.scalar_tensor_tensor(dz[:, 2 * i:2 * i + 2, :], dzt[:, 2 * i:2 * i + 2, :], 1.0, pairs(ps),
                                       ALU.add, ALU.mult).then_inc(free, 1)
            roots = [0]

            def inverse_root(name):
                copied(dve, name)
                rr = rt2[:, roots[0] % 2, :, :]
                roots[0] += 1
                link(V.reciprocal(rr, rr))
                return rr

            for r in range(3):
                rr = inverse_root(f"qn{r}")
                z = PAIRS[r][0]
                V.scalar_tensor_tensor(z, z, wq8 if r < 2 else col("k_norm"), rr, ALU.mult, ALU.mult).then_inc(l2_ready, 1)
            for r in range(3):
                if r:
                    dve.wait_ge(rot_ready, 7 + r)
                z = PAIRS[r][0]
                dve.wait_ge(l2_ready, r + 1)
                rotate(f"rotg{r}", z, z, "cos2", "sin2", ra2, rb2)
            for r in range(4):
                rr = inverse_root(f"l2{r}")
                z = DPAIRS[r][0]
                dve.wait_ge(cvs_ready, r // 2 + 1)
                V.scalar_tensor_tensor(z, z, 0.0625 if r < 2 else 0.5, rr, ALU.mult, ALU.mult).then_inc(l2_ready, 1)
            attention("gqa")
            ps, free = full(dve, "gc")
            V.tensor_copy(gct, ps[:, 0:32].rearrange("p (t n) -> p t n", t=2))
            V.tensor_copy(sp_a[0], ps[:, 32:64].rearrange("p (t n) -> p t n", t=2)).then_inc(free, 1)
            copied(dve, "gc")
            V.tensor_tensor(ekd, sp_a[0], gct, ALU.subtract).then_inc(ekd_ready, 1)
            dve.wait_ge(ekx_ready, 1)
            copied(dve, "tok00", "tok01", "tok10", "tok11")

            def dt(v):
                return v.rearrange("p (d t) c -> p d t c", d=2)

            for h0 in range(0, 8, 2):
                pair = (h0, h0 + 1)
                for h in pair:
                    e = h % 2
                    ps, _ = full(dve, f"gr{h}")
                    for j in range(4):
                        d, t = j // 2, j % 2
                        ins = V.scalar_tensor_tensor(d_LT[e][:, j, :], ps[:, j * P:(j + 1) * P],
                                                     gct[:, t, 8 * d + h:8 * d + h + 1], neg[:, d, :], ALU.subtract, ALU.add)
                    ins.then_inc(dd_ready, 1)
                for h in pair:
                    e = h % 2
                    ps, free = full(dve, f"kk{h}")
                    dve.wait_ge(dec_ready, h + 1)
                    if h0:
                        full(dve, f"do{h - 2}")
                    kq = ps[:, 2 * P:4 * P].rearrange("p (t c) -> p t c", t=2).unsqueeze(1).broadcast_to([P, 2, 2, P])
                    link(V.tensor_tensor(dt(d_AT[e]), kq, dt(d_LT[e]), ALU.mult))
                    for j in range(4):
                        d, t = j // 2, j % 2
                        ins = V.scalar_tensor_tensor(d_LT[e][:, j, :], ps[:, t * P:(t + 1) * P],
                                                     beta[:, t, 8 * d + h:8 * d + h + 1], d_LT[e][:, j, :], ALU.mult, ALU.mult)
                    ins.then_inc(free, 1)
                    for d in range(2):
                        ins = V.tensor_scalar(d_kd[e][:, d, :], ktok[:, d, h * HD:(h + 1) * HD],
                                              ekd[:, d, 8 * d + h:8 * d + h + 1], None, ALU.mult)
                    ins.then_inc(kd_ready, 1)
                for i, h in enumerate(pair):
                    e = h % 2
                    dve.wait_ge(LM_ready, NLEV * h0 + i + 1)
                    V.tensor_tensor(d_TT[e], ident.unsqueeze(1).broadcast_to([P, 4, P]), d_LM[e], ALU.subtract
                                    ).then_inc(TT_ready, 1)
                for l in range(1, NLEV):
                    for h in pair:
                        e = h % 2
                        if l < NLEV - 1:
                            ps, free = full(dve, f"TX{h}_{l}")
                            copied(dve, f"T0_{h}")
                            V.tensor_tensor(d_T[e], d_T[e], fours(ps), ALU.subtract).then_inc(free, 1)
                        ps, free = full(dve, f"XT{h}_{l}")
                        V.tensor_tensor(d_TT[e], d_TT[e], fours(ps), ALU.subtract).then_inc(free, 1)
                for h in pair:
                    ps, free = full(dve, f"vn{h}")
                    for d in range(2):
                        ins = V.tensor_scalar(d_vn[h % 2][:, 2 * d + d, :], ps[:, d * HD:(d + 1) * HD],
                                              beta[:, d, 8 * d + h:8 * d + h + 1], None, ALU.mult)
                    ins.then_inc(free, 1)
                for h in pair:
                    ps, free = full(dve, f"ks{h}")
                    for d in range(2):
                        ins = V.tensor_tensor(d_v2[h % 2][:, d, :], vtok[:, second(d), h * HD:(h + 1) * HD],
                                              ps[:, d * HD:(d + 1) * HD], ALU.subtract)
                    ins.then_inc(free, 1)
                for h in pair:
                    ps, free = full(dve, f"vm{h}")
                    for d in range(2):
                        t = second(d)
                        ins = V.tensor_scalar(d_vn[h % 2][:, 2 * d + t, :], ps[:, d * HD:(d + 1) * HD],
                                              beta[:, t, 8 * d + h:8 * d + h + 1], None, ALU.mult)
                    ins.then_inc(free, 1)
            for r in range(2):
                rr = inverse_root(f"on{r}")
                o = d_o[:, 2 * r:2 * r + 2, :]
                link(V.scalar_tensor_tensor(o, o, col("dn_norm"), rr, ALU.mult, ALU.mult))
                V.scalar_tensor_tensor(dnT[:, 2 * r:2 * r + 2, :], o, 0.5, dz[:, 2 * r:2 * r + 2, :],
                                       ALU.mult, ALU.mult).then_inc(dn_ready, 1)
            for tag, dst in (("au", sga), ("du", sgd)):
                for b in range(4):
                    ps, free = full(dve, f"{tag}{b}")
                    z = dst[:, 2 * b:2 * b + 2, :]
                    n = b + (0 if tag == "au" else 4)
                    copied(dve, f"sg{n // 2}_{n % 2}")
                    V.scalar_tensor_tensor(z, z, 1.0, pairs(ps), ALU.add, ALU.mult).then_inc(free, 1)
                    if tag == "du":
                        copied(dve, f"du{b}", f"au{b}")
                        V.tensor_tensor(sga[:, 2 * b:2 * b + 2, :], sga[:, 2 * b:2 * b + 2, :], z, ALU.add).then_inc(mg_ready, 1)
            for i in range(4):
                ps, free = full(dve, f"wo{i // 2}_{i % 2}")
                for j in range(2):
                    c = 2 * i + j
                    ins = V.scalar_tensor_tensor(xT[:, c, :], ps[:, j * S:(j + 1) * S], hgt1[:, c:c + 1], xT[:, c, :],
                                                 ALU.mult, ALU.add)
                ins.then_inc(free, 1)
            shifted_norm("n2", g2s, 24)
            ps, _ = full(dve, "router")
            V.tensor_reduce(nmx[:, 0, :], ps[:, 0:32].rearrange("p (t n) -> p t n", t=2), AX.X, ALU.max,
                            negate=True).then_inc(rt_mx, 1)
            copied(dve, "router")
            link(V.reciprocal(raff, raff))
            for t in range(TT):
                ins = V.tensor_scalar(aff[:, t, :], aff[:, t, :], raff[:, t:t + 1], None, ALU.mult)
            ins.then_inc(aff_ready, 1)
            ps, free = full(dve, "affT")
            V.tensor_copy(rw[0], ps[0:NE, 0:S])
            V.tensor_copy(rw[1], ps[0:NE, 0:S]).then_inc(free, 1)
            copied(dve, "affT")
            for r in range(CAP // 8):
                link(V.max(top8[0:NE, :], rw[1]))
                link(V.match_replace(rw[1], top8[0:NE, :], rw[1], -1.0))
            link(V.tensor_tensor(rw[3], rw[1], rw[0], ALU.not_equal))
            link(V.tensor_tensor_scan(rw[2], rw[3], rw[3], 0.0, ALU.add, ALU.max))
            link(V.tensor_tensor(rw[2], rw[2], rw[3], ALU.mult))
            V.tensor_scalar(rw[2], rw[2], -1.0, None, ALU.add).then_inc(sel_ready, 1)
            ps, free = full(dve, "selT")
            V.tensor_copy(selc, ps[:, 0:32].rearrange("p (t n) -> p t n", t=2)).then_inc(free, 1)
            copied(dve, "selT")

            def by_slot(v):
                return v.unsqueeze(2).broadcast_to([P, NE, CAP])

            for t in range(TT):
                ins = V.tensor_tensor(Ph[:, t, :].rearrange("p (e r) -> p e r", e=NE),
                                      con("slot").unsqueeze(1).broadcast_to([P, NE, CAP]), by_slot(selc[:, t, :]), ALU.is_equal)
            ins.then_inc(P_ready, 1)
            dve.wait_ge(P_ready, 1)
            for t in range(TT):
                ins = V.tensor_tensor(Pg[:, t, :].rearrange("p (e r) -> p e r", e=NE),
                                      Ph[:, t, :].rearrange("p (e r) -> p e r", e=NE), by_slot(aff[:, t, :]), ALU.mult)
            ins.then_inc(PG_ready, 1)
            for c in range(1, DC, 2):
                ps, free = full(dve, f"xe{c}")
                V.tensor_copy(xe[:, c, :], ps).then_inc(free, 1)
            V.nop().then_inc(hg_ready, 1)
            with dve.Fori(0, NE) as e:
                dve.wait_ge(eth_ready, e + 1)
                link_gate = V.scalar_tensor_tensor(tg, tg, 1.0, pb[:, 4, 0:S].rearrange("p (c n) -> p c n", n=CAP),
                                                   ALU.add, ALU.mult)
                link_gate.then_inc(eg_ready, 1)
                dve.wait_ge(eg_ready, e + 1)
                dve.wait_ge(filled[5], e * 2 + (EMARK[5] + 2))
                V.scalar_tensor_tensor(hg, tg, 0.5, pb[:, 5, 0:S].rearrange("p (c n) -> p c n", n=CAP),
                                       ALU.mult, ALU.mult).then_inc(hg_ready, 1)
            for g in range(4):
                ps, free = full(dve, f"yt{g}1")
                V.tensor_copy(ytok[:, g, 512:1024], ps).then_inc(free, 1)
            for i in range(4):
                ps, free = full(dve, f"fin{i}")
                for j in range(2):
                    c = 2 * i + j
                    ins = V.scalar_tensor_tensor(xT[:, c, :], ps[:, j * S:(j + 1) * S], modc[:, 40 + c:41 + c], xT[:, c, :],
                                                 ALU.mult, ALU.add)
                ins.then_inc(free, 1)


def kernel(**inputs):
    import concourse.bacc as bacc
    from concourse.bass_utils import run_bass_kernel_spmd

    a = {k: np.asarray(v) for k, v in inputs.items()}

    def as_cols(v):
        return v.reshape(-1, P).T

    def spread(v):
        return np.broadcast_to(v.reshape(1, -1), (P, v.size))

    packed = {
        "ab_norm": as_cols(a["ab_norm"]), "cd_norm": as_cols(a["cd_norm"]),
        "xa_norm0": as_cols(a["xa_norm"][0]), "xa_norm1": as_cols(a["xa_norm"][1]),
        "mem_norm0": as_cols(a["xa_mem_norm"][0]), "mem_norm1": as_cols(a["xa_mem_norm"][1]),
        "mlp_norm0": as_cols(a["mlp_norm"][0]), "mlp_norm1": as_cols(a["mlp_norm"][1]),
        "final_norm": as_cols(a["final_norm"]), "norm1": as_cols(a["norm1_w_2"]), "norm2": as_cols(a["norm2_w_2"]),
        "conv_w": as_cols(a["ab_conv_w"]), "conv_b": as_cols(a["ab_conv_b"]),
        "b_a": as_cols(a["lru_b_a"]), "b_i": as_cols(a["lru_b_i"]), "lam": as_cols(a["lru_lambda"]),
        "c": as_cols(a["c_2"]), "b_ada": as_cols(a["b_ada_2"]), "conv2_w": as_cols(a["conv_w_2"]),
        "q_norm": as_cols(np.tile(a["q_norm_w_2"].ravel(), 2)), "k_norm": as_cols(np.tile(a["k_norm_w_2"].ravel(), 2)),
        "dn_norm": as_cols(np.tile(a["dn_norm_w_2"].ravel(), 2)),
        "fox_b": as_cols(np.concatenate([a["fox_b_f"].ravel(), np.zeros(P - 8, np.float32)])),
        "sink": spread(a["cd_sink"]), "a_log": spread(a["a_log_2"]), "dt_bias": spread(a["dt_bias_2"]),
    }
    lru_w = np.zeros((P, 8, P), np.float32)
    for i, w in enumerate((a["lru_w_a"][0], a["lru_w_i"][0])):
        for c in range(4):
            for b in range(2):
                lru_w[64 * b:64 * b + 64, 4 * i + c, 64 * b:64 * b + 64] = w[2 * c + b]

    def as_chunks(w):
        return w.reshape(DC, P, -1).transpose(1, 0, 2).reshape(P, -1)

    def grouped(w):
        return np.concatenate([w[:, 0:64], w[:, 0:64], w[:, 64:128], w[:, 64:128], w[:, 128:256]], axis=1)

    arrays = {
        "cd_w_kv": grouped(a["cd_w_in"][0][:, 2048:2304]), "w_kv_2": grouped(a["w_in_2"][0][:, 512:768]),
        "xT": np.ascontiguousarray(a["x"][0].T), "memT": np.ascontiguousarray(a["mem"][0].T),
        "cols": np.ascontiguousarray(np.concatenate([packed[n] for n in COLS], axis=1)),
        "cons": constants(),
        "small_w": np.ascontiguousarray(np.concatenate([
            as_chunks(a["ab_w_in"][0][:, 2560:2568]), as_chunks(a["w_in_2"][0][:, 2816:2848]),
            as_chunks(a["w_router_2"][0])], axis=1)),
        "lru_w": lru_w.reshape(P, -1),
    }
    for name in ("ab_w_in", "ab_w_out", "cd_w_in", "cd_w_out", "w_ada_2", "w_in_2", "w_attn_up_2", "w_dn_up_2",
                 "w_o_2", "w_gate_2", "w_up_2", "w_down_2"):
        arrays[name] = a[name][0]
    for name in ("xa_w_q", "xa_w_kv", "xa_w_o", "mlp_w_up", "mlp_w_down"):
        arrays[name] = a[name]

    nc = bacc.Bacc("TRN2", target_bir_lowering=False, num_devices=1)
    feeds = {f"in_{k}": np.ascontiguousarray(v) for k, v in arrays.items()}
    aps = {k: nc.dram_tensor(f"in_{k}", v.shape, F32, kind="ExternalInput").ap() for k, v in arrays.items()}
    out = nc.dram_tensor("out", (D, S), F32, kind="ExternalOutput").ap()
    program(nc, aps, out)
    r = run_bass_kernel_spmd(nc, [feeds], core_ids=[0])
    return np.ascontiguousarray(r.results[0]["out"].T)[None]
```
